# Optimizing a Trainium2 kernel written in Bass

```python
import math
import jax, jax.numpy as jnp
from jax import lax
import numpy as np

D_MODEL = 1024
BATCH = 1
SEQ = 512
DEPTH = 2
DEC_BATCH = 8
DEC_SEQ = 8
PAST_LEN = 2048
PAGE_SIZE = 128

N_A_LAYERS = DEPTH // 2
N_B_LAYERS = DEPTH - N_A_LAYERS
D_FF = 2816
EXPAND = 2
D_INNER = EXPAND * D_MODEL
SSM_HEAD_DIM = 64
SSM_HEADS = D_INNER // SSM_HEAD_DIM
SSM_GROUPS = 4
SSM_D_STATE = 128
CONV_WIDTH = 4
CONV_DIM = D_INNER + 2 * SSM_GROUPS * SSM_D_STATE
D_IN_PROJ = D_INNER + CONV_DIM + SSM_HEADS
SSD_CHUNK = 128
WINDOW = 128
ATT_HEAD_DIM = 64
N_Q_HEADS = D_MODEL // ATT_HEAD_DIM
N_KV_HEADS = 4
Q_PER_KV = N_Q_HEADS // N_KV_HEADS
NORM_EPS = 1e-5

kernel_name = 'hybrid_ssd_swa_yoco_step'

def rmsnorm(x, g):
    xf = x.astype(jnp.float32)
    y = xf * lax.rsqrt(jnp.mean(xf * xf, axis=-1, keepdims=True) + NORM_EPS)
    return (y * g.astype(jnp.float32)).astype(x.dtype)

def swiglu(h, w_gu, w_down):
    g, u = jnp.split(h @ w_gu, 2, axis=-1)
    return (jax.nn.silu(g) * u) @ w_down

def alibi_slopes():
    i = jnp.arange(1, N_Q_HEADS + 1, dtype=jnp.float32)
    return (2.0 ** (-8.0 * i / N_Q_HEADS)).reshape(N_KV_HEADS, Q_PER_KV)

def ssd_scan(x, dt, a, b_in, c_in, h0):
    bsz, L = x.shape[0], x.shape[1]
    l = SSD_CHUNK if L % SSD_CHUNK == 0 else L
    nc = L // l
    G, R = SSM_GROUPS, SSM_HEADS // SSM_GROUPS
    P, N = SSM_HEAD_DIM, SSM_D_STATE
    x = x.reshape(bsz, nc, l, G, R, P)
    dt = dt.reshape(bsz, nc, l, G, R)
    bm = b_in.reshape(bsz, nc, l, G, N)
    cm = c_in.reshape(bsz, nc, l, G, N)
    acs = jnp.cumsum(dt * a.reshape(G, R), axis=2)
    xdt = x * dt[..., None]
    at = jnp.moveaxis(acs, 2, -1)
    seg = at[..., :, None] - at[..., None, :]
    causal = jnp.tril(jnp.ones((l, l), dtype=bool))
    decay = jnp.exp(jnp.where(causal, seg, -jnp.inf))
    cb = jnp.einsum('bctgn,bcsgn->bcgts', cm, bm)
    y_diag = jnp.einsum('bcgrts,bcsgrp->bctgrp', cb[:, :, :, None] * decay, xdt)
    decay_s = jnp.exp(acs[:, :, -1:] - acs)
    states = jnp.einsum('bcsgn,bcsgr,bcsgrp->bcgrpn', bm, decay_s, xdt)
    chunk_decay = jnp.exp(acs[:, :, -1])

    def step(h, inp):
        s_c, d_c = inp
        return h * d_c[..., None, None] + s_c, h

    h_fin, h_in = lax.scan(step, h0.reshape(bsz, G, R, P, N),
                           (jnp.moveaxis(states, 1, 0), jnp.moveaxis(chunk_decay, 1, 0)))
    h_in = jnp.moveaxis(h_in, 0, 1)
    y_off = jnp.einsum('bctgn,bcgrpn,bctgr->bctgrp', cm, h_in, jnp.exp(acs))
    y = (y_diag + y_off).reshape(bsz, L, SSM_HEADS, P)
    return y, h_fin.reshape(bsz, SSM_HEADS, P, N)

def mamba2_mixer(h, w_in, conv_w, conv_b, dt_bias, a_log, d_skip, gate_norm, w_out, ssm0, conv0):
    bsz, L = h.shape[0], h.shape[1]
    f32 = jnp.float32
    proj = h @ w_in
    z = proj[..., :D_INNER]
    xbc = proj[..., D_INNER:D_INNER + CONV_DIM]
    dt_raw = proj[..., D_INNER + CONV_DIM:]
    xin = jnp.concatenate([conv0.astype(xbc.dtype), xbc], axis=1)
    conv_new = xin[:, L:]
    xc = conv_b + sum(xin[:, k:k + L] * conv_w[k] for k in range(CONV_WIDTH))
    xc = jax.nn.silu(xc)
    gn = SSM_GROUPS * SSM_D_STATE
    xs = xc[..., :D_INNER].reshape(bsz, L, SSM_HEADS, SSM_HEAD_DIM).astype(f32)
    bm = xc[..., D_INNER:D_INNER + gn].reshape(bsz, L, SSM_GROUPS, SSM_D_STATE).astype(f32)
    cm = xc[..., D_INNER + gn:].reshape(bsz, L, SSM_GROUPS, SSM_D_STATE).astype(f32)
    dt = jax.nn.softplus(dt_raw.astype(f32) + dt_bias.astype(f32))
    a = -jnp.exp(a_log.astype(f32))
    y, h_fin = ssd_scan(xs, dt, a, bm, cm, ssm0.astype(f32))
    y = y + d_skip.astype(f32)[:, None] * xs
    y = y.reshape(bsz, L, D_INNER) * jax.nn.silu(z.astype(f32))
    yg = y.reshape(bsz, L, SSM_GROUPS, D_INNER // SSM_GROUPS)
    yg = yg * lax.rsqrt(jnp.mean(yg * yg, axis=-1, keepdims=True) + NORM_EPS)
    y = yg.reshape(bsz, L, D_INNER) * gate_norm.astype(f32)
    out = y.astype(h.dtype) @ w_out
    return out, h_fin.astype(ssm0.dtype), conv_new

def sink_alibi_attention(q, k, v, dist, valid, sinks):
    s = jnp.einsum('...qkgd,...skd->...kgqs', q, k).astype(jnp.float32) * (ATT_HEAD_DIM ** -0.5)
    s = s - alibi_slopes()[:, :, None, None] * dist
    s = jnp.where(valid, s, -jnp.inf)
    sink_col = jnp.broadcast_to(sinks.astype(jnp.float32).reshape(N_KV_HEADS, Q_PER_KV)[:, :, None, None],
                                s.shape[:-1] + (1,))
    p = jax.nn.softmax(jnp.concatenate([s, sink_col], axis=-1), axis=-1)[..., :-1]
    return jnp.einsum('...kgqs,...skd->...qkgd', p.astype(v.dtype), v)

def swa_prompt(q, k, v, sinks):
    bsz, L = q.shape[0], q.shape[1]
    nb = L // WINDOW
    qb = q.reshape(bsz, nb, WINDOW, N_KV_HEADS, Q_PER_KV, ATT_HEAD_DIM)

    def band(t):
        tb = t.reshape(bsz, nb, WINDOW, N_KV_HEADS, ATT_HEAD_DIM)
        prev = jnp.concatenate([jnp.zeros_like(tb[:, :1]), tb[:, :-1]], axis=1)
        return jnp.concatenate([prev, tb], axis=2)

    qi = WINDOW + jnp.arange(WINDOW)
    kj = jnp.arange(2 * WINDOW)
    dist = qi[:, None] - kj[None, :]
    kabs = jnp.arange(nb)[:, None] * WINDOW - WINDOW + kj[None, :]
    valid = (dist >= 0) & (dist < WINDOW) & (kabs[:, None, None, None, :] >= 0)
    o = sink_alibi_attention(qb, band(k), band(v), dist.astype(jnp.float32), valid, sinks)
    return o.reshape(bsz, L, N_Q_HEADS * ATT_HEAD_DIM)

def swa_sample(q, k_all, v_all, sinks):
    bsz, T = q.shape[0], q.shape[1]
    Tk = k_all.shape[1]
    qb = q.reshape(bsz, T, N_KV_HEADS, Q_PER_KV, ATT_HEAD_DIM)
    qi = WINDOW + jnp.arange(T)
    kj = jnp.arange(Tk)
    dist = qi[:, None] - kj[None, :]
    kabs = PAST_LEN - WINDOW + kj
    valid = (dist >= 0) & (dist < WINDOW) & (kabs[None, :] >= 0)
    o = sink_alibi_attention(qb, k_all, v_all, dist.astype(jnp.float32), valid, sinks)
    return o.reshape(bsz, T, N_Q_HEADS * ATT_HEAD_DIM)

def trunk(x, ssm_in, conv_in, k_buf, v_buf, p):
    is_prompt = k_buf is None
    bsz, L = x.shape[0], x.shape[1]
    ssm_out, conv_out = [], []
    k_all = v_all = None
    for layer in range(DEPTH):
        if layer == N_A_LAYERS:
            kv = rmsnorm(x, p['kv_norm']) @ p['w_kv']
            nkv = N_KV_HEADS * ATT_HEAD_DIM
            k_new = kv[..., :nkv].reshape(bsz, L, N_KV_HEADS, ATT_HEAD_DIM)
            v_new = kv[..., nkv:].reshape(bsz, L, N_KV_HEADS, ATT_HEAD_DIM)
            if is_prompt:
                k_all, v_all = k_new, v_new
            else:
                k_all = jnp.concatenate([k_buf.astype(k_new.dtype), k_new], axis=1)
                v_all = jnp.concatenate([v_buf.astype(v_new.dtype), v_new], axis=1)
        x = x + 0.5 * swiglu(rmsnorm(x, p['ffn1_norm'][layer]), p['ffn1_w_gu'][layer], p['ffn1_w_down'][layer])
        h = rmsnorm(x, p['mix_norm'][layer])
        if layer < N_A_LAYERS:
            i = layer
            out, s_f, c_f = mamba2_mixer(h, p['ssm_w_in'][i], p['ssm_conv_w'][i], p['ssm_conv_b'][i],
                                         p['ssm_dt_bias'][i], p['ssm_a_log'][i], p['ssm_d'][i],
                                         p['ssm_gate_norm'][i], p['ssm_w_out'][i], ssm_in[i], conv_in[i])
            ssm_out.append(s_f)
            conv_out.append(c_f)
        else:
            j = layer - N_A_LAYERS
            q = (h @ p['attn_w_q'][j]).reshape(bsz, L, N_Q_HEADS, ATT_HEAD_DIM)
            if is_prompt:
                o = swa_prompt(q, k_all, v_all, p['attn_sinks'][j])
            else:
                o = swa_sample(q, k_all, v_all, p['attn_sinks'][j])
            out = o @ p['attn_w_o'][j]
        x = x + out
        x = x + 0.5 * swiglu(rmsnorm(x, p['ffn2_norm'][layer]), p['ffn2_w_gu'][layer], p['ffn2_w_down'][layer])
    y = rmsnorm(x, p['final_norm'])
    return y, jnp.stack(ssm_out), jnp.stack(conv_out), k_all[:, -WINDOW:], v_all[:, -WINDOW:]

def setup_inputs(seed: int = 0) -> dict:
    key = jax.random.key(seed)
    ks = iter(jax.random.split(key, 32))
    f32 = jnp.float32

    def nrm(shape, scale):
        return jax.random.normal(next(ks), shape, f32) * scale

    def gain(shape):
        return 1.0 + 0.05 * jax.random.normal(next(ks), shape, f32)

    dt0 = jnp.exp(jax.random.uniform(next(ks), (N_A_LAYERS, SSM_HEADS), f32,
                                     math.log(1e-3), math.log(1e-1)))
    return {
        'x_prompt': nrm((BATCH, SEQ, D_MODEL), 1.0),
        'x_sample': nrm((DEC_BATCH, DEC_SEQ, D_MODEL), 1.0),
        'state_ssm': nrm((N_A_LAYERS, DEC_BATCH, SSM_HEADS, SSM_HEAD_DIM, SSM_D_STATE), 0.1),
        'state_conv': nrm((N_A_LAYERS, DEC_BATCH, CONV_WIDTH - 1, CONV_DIM), 1.0),
        'cache_k_win': nrm((DEC_BATCH, WINDOW, N_KV_HEADS, ATT_HEAD_DIM), 1.0),
        'cache_v_win': nrm((DEC_BATCH, WINDOW, N_KV_HEADS, ATT_HEAD_DIM), 1.0),
        'ffn1_norm': gain((DEPTH, D_MODEL)),
        'ffn1_w_gu': nrm((DEPTH, D_MODEL, 2 * D_FF), D_MODEL ** -0.5),
        'ffn1_w_down': nrm((DEPTH, D_FF, D_MODEL), D_FF ** -0.5),
        'mix_norm': gain((DEPTH, D_MODEL)),
        'ffn2_norm': gain((DEPTH, D_MODEL)),
        'ffn2_w_gu': nrm((DEPTH, D_MODEL, 2 * D_FF), D_MODEL ** -0.5),
        'ffn2_w_down': nrm((DEPTH, D_FF, D_MODEL), D_FF ** -0.5),
        'ssm_w_in': nrm((N_A_LAYERS, D_MODEL, D_IN_PROJ), D_MODEL ** -0.5),
        'ssm_conv_w': jax.random.uniform(next(ks), (N_A_LAYERS, CONV_WIDTH, CONV_DIM), f32, -0.5, 0.5),
        'ssm_conv_b': nrm((N_A_LAYERS, CONV_DIM), 0.02),
        'ssm_dt_bias': dt0 + jnp.log(-jnp.expm1(-dt0)),
        'ssm_a_log': jnp.log(jax.random.uniform(next(ks), (N_A_LAYERS, SSM_HEADS), f32, 1.0, 16.0)),
        'ssm_d': gain((N_A_LAYERS, SSM_HEADS)),
        'ssm_gate_norm': gain((N_A_LAYERS, D_INNER)),
        'ssm_w_out': nrm((N_A_LAYERS, D_INNER, D_MODEL), D_INNER ** -0.5),
        'kv_norm': gain((D_MODEL,)),
        'w_kv': nrm((D_MODEL, 2 * N_KV_HEADS * ATT_HEAD_DIM), D_MODEL ** -0.5),
        'attn_w_q': nrm((N_B_LAYERS, D_MODEL, N_Q_HEADS * ATT_HEAD_DIM), D_MODEL ** -0.5),
        'attn_sinks': nrm((N_B_LAYERS, N_Q_HEADS), 0.5),
        'attn_w_o': nrm((N_B_LAYERS, N_Q_HEADS * ATT_HEAD_DIM, D_MODEL), (N_Q_HEADS * ATT_HEAD_DIM) ** -0.5),
        'final_norm': gain((D_MODEL,)),
    }

def reference(x_prompt, x_sample, state_ssm, state_conv, cache_k_win, cache_v_win,
              ffn1_norm, ffn1_w_gu, ffn1_w_down, mix_norm, ffn2_norm, ffn2_w_gu, ffn2_w_down,
              ssm_w_in, ssm_conv_w, ssm_conv_b, ssm_dt_bias, ssm_a_log, ssm_d, ssm_gate_norm, ssm_w_out,
              kv_norm, w_kv, attn_w_q, attn_sinks, attn_w_o, final_norm):
    p = dict(ffn1_norm=ffn1_norm, ffn1_w_gu=ffn1_w_gu, ffn1_w_down=ffn1_w_down, mix_norm=mix_norm,
             ffn2_norm=ffn2_norm, ffn2_w_gu=ffn2_w_gu, ffn2_w_down=ffn2_w_down,
             ssm_w_in=ssm_w_in, ssm_conv_w=ssm_conv_w, ssm_conv_b=ssm_conv_b, ssm_dt_bias=ssm_dt_bias,
             ssm_a_log=ssm_a_log, ssm_d=ssm_d, ssm_gate_norm=ssm_gate_norm, ssm_w_out=ssm_w_out,
             kv_norm=kv_norm, w_kv=w_kv, attn_w_q=attn_w_q, attn_sinks=attn_sinks, attn_w_o=attn_w_o,
             final_norm=final_norm)
    bp = x_prompt.shape[0]
    ssm0 = jnp.zeros((N_A_LAYERS, bp, SSM_HEADS, SSM_HEAD_DIM, SSM_D_STATE), x_prompt.dtype)
    conv0 = jnp.zeros((N_A_LAYERS, bp, CONV_WIDTH - 1, CONV_DIM), x_prompt.dtype)
    y_prompt, ssm_p, conv_p, kw_p, vw_p = trunk(x_prompt, ssm0, conv0, None, None, p)
    y_sample, ssm_s, conv_s, kw_s, vw_s = trunk(x_sample, state_ssm, state_conv, cache_k_win, cache_v_win, p)
    return (y_prompt, y_sample, ssm_p, conv_p, kw_p, vw_p, ssm_s, conv_s, kw_s, vw_s)


_drawn_inputs = setup_inputs


def setup_inputs(seed=0):
    import zlib

    import numpy as np

    out = dict(_drawn_inputs(seed))
    spreads = {}
    factors = {'ffn2_norm': 2.807, 'attn_sinks': 3.584}
    for name, (base, spread) in spreads.items():
        noise = np.random.default_rng([zlib.crc32(name.encode()), seed]).standard_normal(out[name].shape)
        drawn = base * np.exp(spread * noise) if base else spread * noise
        out[name] = __import__('jax').numpy.asarray(drawn.astype(out[name].dtype))
    for name, factor in factors.items():
        out[name] = (out[name] * factor).astype(out[name].dtype)
    return out
```

```python
from contextlib import ExitStack

import numpy as np
import concourse.bass as bass
from concourse import mybir

F32 = mybir.dt.float32
F32R = mybir.dt.float32r
ALU = mybir.AluOpType
ACT = mybir.ActivationFunctionType

P = 128
D_MODEL, D_FF = 1024, 2816
SEQ, DEC_BATCH, DEC_SEQ = 512, 8, 8
S = DEC_BATCH * DEC_SEQ
T = SEQ + S
HALF = T // 2
NK = D_MODEL // P
NF = D_FF // P
D_INNER, HEADS, HEAD_DIM, GROUPS, D_STATE = 2048, 32, 64, 4, 128
CONV = 4
NX = D_INNER // P
NXBC = NX + 2 * GROUPS
L = 128
NC = SEQ // L
KVH, QH, HD, WINDOW = 4, 16, 64, 128
EPS = 1e-5
UNIT = 8
PAST = 2048

G_FFN1, G_MIX, G_FFN2, G_KV, G_FINAL = 0, 16, 32, 48, 56
G_GATE, G_D, G_CONVB, G_CONVW = 64, 80, 96, 120
NPARAM = G_CONVW + CONV * NXBC
C_ONES, C_IDENT, C_TRI, C_STRICT, C_TRI_S, C_STRICT_S, C_BLOCK = 0, 128, 256, 384, 512, 577, 641
NCONST = 649
KS = WINDOW + DEC_SEQ
NEGD, BIAS_S, SLOPE, SINK, SINK_S = 0, 2 * L, 2 * L + KS, 2 * L + KS + QH, 2 * L + KS + 2 * QH
NATT = SINK_S + 1
MASKED = -1e30
CBUF = 3 + SEQ + DEC_BATCH * (3 + DEC_SEQ)
CLEN = CBUF - 3
ES = SEQ + S + 4


def down_widths(k_tiles):
    return [min(UNIT, k_tiles - a) for a in range(0, k_tiles, UNIT)]


def unit_plan():
    plan, n = {}, 0
    for name, units in [("gu0", 2 * NF), ("down0", NK * 3), ("dt", 1), ("bc", 2 * GROUPS), ("xz", 2 * NX),
                        ("out", NK * 2), ("gu1", 2 * NF), ("down1", NK * 3), ("kv", 4), ("gu2", 2 * NF),
                        ("down2", NK * 3), ("q", NK), ("o", NK), ("gu3", 2 * NF), ("down3", NK * 3)]:
        plan[name] = n
        n += units
    plan["end"] = n
    return plan


PLAN = unit_plan()


def tile_plan():
    plan, m = {}, 0
    for name, tiles in [("gu0", 2 * NF), ("down0", NK), ("dt", 1), ("bc", 2 * GROUPS + 1), ("xz", 2 * NX), ("out", NK),
                        ("gu1", 2 * NF), ("down1", NK), ("kv", 4), ("gu2", 2 * NF), ("down2", NK), ("q", NK),
                        ("o", NK), ("gu3", 2 * NF), ("down3", NK)]:
        plan[name] = m
        m += tiles
    return plan


TILE = tile_plan()
XG = {"gu0": 0, "dt": 1, "gu1": 2, "kv": 3, "gu2": 4, "q": 5, "gu3": 6}
NORM = {"gu0": 0, "dt": 1, "gu1": 2, "kv": 3, "q": 4, "gu3": 5, "final": 6}


SBUF_BASE, SBUF_END = 16512, 229344


class Map:

    def __init__(self, nc, at):
        self.nc, self.at = nc, at

    def __call__(self, name, shape, dt=F32):
        t = self.nc.alloc_sbuf_tensor_at(name, shape, dt, offset=self.at)
        self.at += -(-4 * int(np.prod(shape[1:])) // 32) * 32
        assert self.at <= SBUF_END, (name, self.at - SBUF_END)
        return t


def build(nc, w, x_in, params, consts, att_consts, dt_params, conv_state, ssm_state, ssm_state_t, cache_kt, cache_v,
          cache_kv, y_out, ssm_p_out, ssm_s_out, conv_p_out, conv_s_out, kwin_p_out, vwin_p_out, kv_kept_out,
          kv_new_out):
    with ExitStack() as ctx:
        sb = Map(nc, SBUF_BASE)
        x = sb("x", [P, NK, T])
        xhi = sb("xhi", [P, NK, T], F32R)
        xlo = sb("xlo", [P, NK, T], F32R)
        wraw = [sb(f"wraw{s}", [P, UNIT * P]) for s in range(2)]
        whi = [sb(f"whi{s}", [P, UNIT * P], F32R) for s in range(2)]
        wlo = [sb(f"wlo{s}", [P, UNIT * P], F32R) for s in range(2)]
        rstd = sb("rstd", [P, T])
        prm = sb("prm", [P, NPARAM])
        cst = sb("cst", [P, NCONST])
        sqsum = sb("sqsum", [P, T])
        sq = sb("sq", [P, T])
        arena = sb.at
        ffn = Map(nc, arena)
        hhi = ffn("hhi", [P, NF, T], F32R)
        hlo = ffn("hlo", [P, NF, T], F32R)
        gate = ffn("gate", [P, T])
        silu = ffn("silu", [P, T])
        up = ffn("up", [P, T])
        hidden = ffn("hidden", [P, T])
        firstsq = nc.alloc_sbuf_tensor_at("firstsq", [P, NK - 1, T], F32, offset=arena + 4 * T * (NF - NK + 1))
        mam = Map(nc, arena)
        yall = mam("yall", [P, NX, T])
        CT = mam("CT", [P, GROUPS, T])
        Btm = mam("Btm", [P, GROUPS, NC + 1, P])
        cbm = mam("cbm", [P, GROUPS, T])
        Bm = mam("Bm", [S, DEC_BATCH, P])
        E = mam("E", [P, 2, ES])
        E2 = mam("E2", [P, T])
        xdt = mam("xdt", [P, NC + 1, P])
        xdd = mam("xdd", [P, NC + 1, P])
        yo = nc.alloc_sbuf_tensor_at("yo", [P, T], F32, offset=mam.at - 4 * P * (NC + 1))
        hT = nc.alloc_sbuf_tensor_at("hT", [P, NC - 1, P], F32, offset=mam.at - 4 * P * (NC + 1))
        hst = mam("hst", [P, NC, P])
        h0s = mam("h0s", [P, DEC_BATCH, P])
        h0T = mam("h0T", [P, DEC_BATCH, P])
        cbuf = mam("cbuf", [P, CBUF])
        cacc = mam("cacc", [P, CBUF])
        th = mam("th", [P, CBUF])
        xs = mam("xs", [P, T])
        yd = sqsum
        gsum = mam("gsum", [P, GROUPS, T])
        dT = mam("dT", [P, NC + 1, 2 * HEADS])
        segL = mam("segL", [P, 2, NC, P])
        segLs = mam("segLs", [S, 2, S])
        pairA = mam("pairA", [P, NC + 1, 2, HEAD_DIM])
        cstate = mam("cstate", [P, NXBC, DEC_BATCH, 3])
        cnew = mam("cnew", [P, NXBC, 3])
        pre = Map(nc, arena)
        BT = pre("BT", [P, GROUPS, T])
        dtp = pre("dtp", [2 * HEADS, T])
        dts = [pre(f"dts{i}", [HEADS, T]) for i in range(5)]
        dtprm = pre("dtprm", [HEADS, 4])
        post = Map(nc, arena)
        ylo = post("ylo", [P, NX, T], F32R)
        yhi = post("yhi", [P, NX, T], F32R)
        ybuf = nc.alloc_sbuf_tensor_at("ybuf", [P, NK, T], F32, offset=arena)

        KVT = ffn("KVT", [P, 4, T])
        att = Map(nc, arena)
        ohi = att("ohi", [P, NK, T], F32R)
        olo = att("olo", [P, NK, T], F32R)
        qs = att("qs", [P, T])
        VT = att("VT", [P, NC, KVH * HD])
        Kwin = att("Kwin", [P, KVH * HD])
        kvsam = att("kvsam", [S, 2 * KVH * HD])
        sc_at = att.at
        sc = att("sc", [P, 2, 2 * SEQ])
        probs = att("probs", [P, 2, 2 * SEQ])
        nmax, rsum, esink, rden = (att(v, [P, 2, NC]) for v in ("nmax", "rsum", "esink", "rden"))
        Qsam = att("Qsam", [HD, KVH, DEC_BATCH, QH // KVH, DEC_SEQ])
        snmax, srsum, sesink, srden = (att(v, [P, DEC_BATCH]) for v in ("snmax", "srsum", "sesink", "srden"))
        attc = att("attc", [P, NATT])
        pt_at = att.at
        PT = att("PT", [P, 2, 2 * NC - 1, P])
        Vsam = att("Vsam", [P, DEC_BATCH, KVH * HD])
        Ksam = att("Ksam", [HD, KVH, DEC_BATCH, KS])
        PTn = att("PTn", [DEC_SEQ, DEC_BATCH, P])
        assert att.at <= arena + 4 * T * (2 * NF + 4)
        psam = nc.alloc_sbuf_tensor_at("psam", [P, DEC_BATCH, KS], F32, offset=sc_at)
        PTs = nc.alloc_sbuf_tensor_at("PTs", [P, DEC_BATCH, P], F32, offset=pt_at)
        Vnew = nc.alloc_sbuf_tensor_at("Vnew", [DEC_SEQ, DEC_BATCH, KVH * HD], F32, offset=SBUF_BASE + 4 * NK * T)
        ssam = nc.alloc_sbuf_tensor_at("ssam", [P, DEC_BATCH, KS], F32, offset=SBUF_BASE + 4 * NK * T + 4 * DEC_BATCH * KVH * HD)
        negd = attc[:, NEGD:NEGD + 2 * L]

        psum = ctx.enter_context(nc.psum_tensor("psum", [P, 8, 512], F32))
        acc = psum[:, 0:4, :]
        nrm = psum[:, 4:6, :]
        bank = [psum[:, b, :] for b in range(8)]

        def sem(name):
            return ctx.enter_context(nc.semaphore(name))

        raw_loaded = [sem("raw_loaded0"), sem("raw_loaded1")]
        weights_hi = sem("weights_hi")
        weights_lo = sem("weights_lo")
        units_done = sem("units_done")
        evicted = sem("evicted")
        x_loaded = [sem(f"x_loaded{k}") for k in range(NK)]
        prm_loaded, c_loaded = sem("prm_loaded"), sem("c_loaded")
        xg_hi = sem("xg_hi")
        xg_used = sem("xg_used")
        xg_lo = sem("xg_lo")
        squared = sem("squared")
        sumsq = sem("sumsq")
        norm_sum = sem("norm_sum")
        var_ready = sem("var_ready")
        std_ready = sem("std_ready")
        rstd_ready = sem("rstd_ready")
        silu_ready = sem("silu_ready")
        h_ready = sem("h_ready")
        h_hi = sem("h_hi")
        h_lo = sem("h_lo")
        y_ready = sem("y_ready")
        conv_prm = sem("conv_prm")
        st_loaded = sem("st_loaded")
        conv_step = sem("conv_step")
        conv_tanh = sem("conv_tanh")
        conv_done = sem("conv_done")
        conv_saved = sem("conv_saved")
        cleared = sem("cleared")
        dt_act = sem("dt_act")
        dt_dve = sem("dt_dve")
        dt_turned = sem("dt_turned")
        dt_kept = sem("dt_kept")
        b_turned, cb_done = sem("b_turned"), sem("cb_done")
        b_kept = sem("b_kept")
        cb_kept = sem("cb_kept")
        bm_ready = sem("bm_ready")
        z_tanh, z_ready = sem("z_tanh"), sem("z_ready")
        seg_lhs = sem("seg_lhs")
        x_turned = sem("x_turned")
        seg_ready = sem("seg_ready")
        decay_ready = sem("decay_ready")
        xdt_ready, xdd_ready = sem("xdt_ready"), sem("xdd_ready")
        m_ready = sem("m_ready")
        s_ready, ss_ready = sem("s_ready"), sem("ss_ready")
        h_step = sem("h_step")
        h0_loaded, h0t_loaded = sem("h0_loaded"), sem("h0t_loaded")
        h0_decayed = sem("h0_decayed")
        ss_final = sem("ss_final")
        h_turned = sem("h_turned")
        hT_ready = sem("hT_ready")
        ssd_done = sem("ssd_done")
        skip_ready = sem("skip_ready")
        y_step = sem("y_step")
        ysq, gsum_step = sem("ysq"), sem("gsum_step")
        hp_stored, hs_stored = sem("hp_stored"), sem("hs_stored")
        cnew_stored = sem("cnew_stored")
        gnorm_sum = sem("gnorm_sum")
        gvar, gstd, grstd = sem("gvar"), sem("gstd"), sem("grstd")
        yn_ready, y_hi, y_lo = sem("yn_ready"), sem("y_hi"), sem("y_lo")
        y_stored = sem("y_stored")

        def out_of(pair):
            return acc[:, 2 * pair:2 * pair + 2, 0:HALF]

        def halves(ap):
            return ap.rearrange("p (a n) -> p a n", a=2)

        kv_turned = sem("kv_turned")
        kv_kept = sem("kv_kept")
        scores_done = sem("scores_done")
        soft = sem("soft")
        p_exp = sem("p_exp")
        den = sem("den")
        p_ready = sem("p_ready")
        p_turned, pt_ready = sem("p_turned"), sem("pt_ready")
        pv_done = sem("pv_done")
        o_hi, o_lo = sem("o_hi"), sem("o_lo")
        qsam_ready = sem("qsam_ready")
        ksam_ready = sem("ksam_ready")
        ssc_done = sem("ssc_done")
        ssoft = sem("ssoft")
        sp_exp, sden, sp_ready = sem("sp_exp"), sem("sden"), sem("sp_ready")
        sp_turned, spt_ready, spv_done = sem("sp_turned"), sem("spt_ready"), sem("spv_done")
        kcache_loaded, vsam_loaded, vnew_loaded = sem("kcache_loaded"), sem("vsam_loaded"), sem("vnew_loaded")
        att_loaded, att_cleared = sem("att_loaded"), sem("att_cleared")
        win_stored, new_stored, cache_moved = sem("win_stored"), sem("new_stored"), sem("cache_moved")

        block = ctx.enter_context(nc.Block())

        def column(at, c, stride=1):
            return prm[:, at + c * stride:at + c * stride + 1] if isinstance(c, int) else prm[:, bass.ds(c * stride + at, 1)]

        def acol(at, head):
            return attc[:, at + head:at + head + 1] if isinstance(head, int) else attc[:, bass.ds(head + at, 1)]

        @block.sync
        def _(sp):
            sp.dma_start(wraw[0][:], w[0]).then_inc(raw_loaded[0], 16)
            for k in range(NK):
                sp.dma_start(x[:, k, :], x_in[:, k, :]).then_inc(x_loaded[k], 16)
                if k == 1:
                    sp.dma_start(wraw[1][:], w[1]).then_inc(raw_loaded[1], 16)
            pairs = (PLAN["end"] - 2) // 2
            with sp.Fori(0, pairs) as i:
                for s in range(2):
                    sp.wait_ge(weights_lo, 2 * i + s + 1)
                    sp.dma_start(wraw[s][:], w[2 * i + 2 + s]).then_inc(raw_loaded[s], 16)
            for n in range(2 * pairs + 2, PLAN["end"]):
                sp.wait_ge(weights_lo, n - 1)
                sp.dma_start(wraw[n % 2][:], w[n]).then_inc(raw_loaded[n % 2], 16)

        ident = cst[:, C_IDENT:C_IDENT + P]
        tri = cst[:, C_TRI:C_TRI + P]
        strict = cst[:, C_STRICT:C_STRICT + P]
        tri_s = cst[0:S, C_TRI_S:C_TRI_S + S + 1]
        strict_s = cst[0:S, C_STRICT_S:C_STRICT_S + S]
        in_seq = cst[0:S, C_BLOCK:C_BLOCK + DEC_BATCH]

        @block.tensor
        def _(pe):
            def unit(n, step, width, pair, hi, lo, k0, start, stop, k_wait=None, norm_after=None, used=None):
                s = n % 2
                pe.wait_ge(weights_lo, n + step + 1)
                last = None
                for k in range(width):
                    if k_wait is not None:
                        pe.wait_ge(k_wait[0], k_wait[1] + k + 1)
                    products = ((whi, hi), (whi, lo), (wlo, hi))
                    for i, (wt, m) in enumerate(products):
                        for half in range(2):
                            last = pe.matmul(acc[:, 2 * pair + half, 0:HALF], wt[s][:, k * P:(k + 1) * P],
                                             m[:, k0 + k, half * HALF:(half + 1) * HALF],
                                             start=start and k == 0 and i == 0,
                                             stop=stop and k == width - 1 and i == 2)
                    if used is not None and k < width - 1:
                        last.then_inc(used, 1)
                    if norm_after is not None and k == 6:
                        norm(norm_after)
                last.then_inc(units_done, 1)

            def half_unit(n, step, pair, part, rhs=(xhi, xlo)):
                s = n % 2
                if part == 0:
                    pe.wait_ge(weights_lo, n + step + 1)
                for k in range(4 * part, 4 * part + 4):
                    for i, (wt, m) in enumerate(((whi, rhs[0]), (whi, rhs[1]), (wlo, rhs[0]))):
                        for half in range(2):
                            last = pe.matmul(acc[:, 2 * pair + half, 0:HALF], wt[s][:, k * P:(k + 1) * P],
                                             m[:, k, half * HALF:(half + 1) * HALF],
                                             start=k == 0 and i == 0, stop=k == NK - 1 and i == 2)
                if part == 1:
                    last.then_inc(units_done, 1)

            def norm(e):
                pe.wait_ge(sumsq, NK * (e + 1))
                if e == 0:
                    pe.wait_ge(c_loaded, 16)
                for half in range(2):
                    last = pe.matmul(nrm[:, half, 0:HALF], cst[:, C_ONES:C_ONES + P], sqsum[:, half * HALF:(half + 1) * HALF],
                                     start=True, stop=True)
                last.then_inc(norm_sum, 1)

            def gate_up(ph, with_norm=True):
                n, m = PLAN[ph], TILE[ph]

                def body(i, first=False):
                    for u in range(2):
                        pe.wait_ge(evicted, m + 2 * i + u + 1)
                        unit(n + u, 2 * i, NK, (m + u) % 2, xhi, xlo, 0, True, True,
                             (xg_lo, NK * XG[ph]) if first and u == 0 else None,
                             norm_after=NORM[ph] if first and u == 0 and with_norm else None)
                body(0, True)
                with pe.Fori(1, NF) as i:
                    body(i)

            def residual(ph, widths, hi, lo, ready, before, kwise=False):
                n, m, per = PLAN[ph], TILE[ph], len(widths)

                def body(i):
                    for d in range(2):
                        pe.wait_ge(evicted, m + 2 * i + d + 1)
                        for a, width in enumerate(widths):
                            if not kwise:
                                pe.wait_ge(ready, before + UNIT * a + width)
                            unit(n + per * d + a, 2 * per * i, width, (m + d) % 2, hi, lo, UNIT * a, a == 0,
                                 a == per - 1)
                if kwise:
                    for a, width in enumerate(widths):
                        for d in range(2):
                            unit(n + 2 * a + d, 0, width, d, hi, lo, UNIT * a, a == 0, a == per - 1,
                                 (ready, before + UNIT * a) if d == 0 else None)
                            if a == d == 0:
                                group_sum(GROUPS - 1, 6)
                with pe.Fori(1 if kwise else 0, NK // 2) as i:
                    body(i)

            def key_value():
                n, m = PLAN["kv"], TILE["kv"]
                for c in range(4):
                    pe.wait_ge(evicted, m + c + 1)
                    unit(n + c, 0, NK, (m + c) % 2, xhi, xlo, 0, True, True,
                         (xg_lo, NK * XG["kv"]) if c == 0 else None, norm_after=NORM["kv"] if c == 0 else None,
                         used=xg_used if c == 3 else None)

            def b_and_c():
                pe.wait_ge(evicted, TILE["dt"] + 1)
                unit(PLAN["dt"], 0, NK, 0, xhi, xlo, 0, True, True, (xg_lo, NK * XG["dt"]), norm_after=NORM["dt"])
                for c in range(2 * GROUPS):
                    pe.wait_ge(evicted, TILE["bc"] + c + 1)
                    unit(PLAN["bc"] + c, 0, NK, (c + 1) % 2, xhi, xlo, 0, True, True)

            def b_c_products():
                pe.wait_ge(rstd_ready, NORM["dt"] + 1)
                for g in range(GROUPS):
                    b = 2 + 3 * (g % 2)
                    pe.wait_ge(conv_done, 2 * (GROUPS + g) + 2)
                    if g == 0:
                        pe.wait_ge(evicted, TILE["xz"] + 3)
                    if g >= 2:
                        pe.wait_ge(b_kept, 2 * g - 2)
                        pe.wait_ge(cb_kept, 2 * g - 2)
                    for c in range(NC):
                        pe.transpose(bank[b][:, c * L:(c + 1) * L], BT[:, g, c * L:(c + 1) * L], ident)
                    pe.transpose(bank[b + 1][0:S, 0:P], BT[:, g, SEQ:T], ident).then_inc(b_turned, 1)
                    for c in range(NC):
                        cols = slice(c * L, (c + 1) * L)
                        pe.matmul(bank[b + 2][:, cols], BT[:, g, cols], CT[:, g, cols], start=True, stop=True)
                    pe.wait_ge(b_kept, 2 * g + 2)
                    pe.matmul(bank[b + 1][0:S, P:P + S], BT[:, g, SEQ:T], CT[:, g, SEQ:T], start=True,
                              stop=True).then_inc(cb_done, 1)

            def turn_dt():
                pe.wait_ge(dt_dve, 7)
                pe.wait_ge(cb_kept, 2 * GROUPS)
                for c in range(NC):
                    pe.transpose(bank[4][:, c * 64:(c + 1) * 64], dtp[:, c * L:(c + 1) * L], ident[0:64, 0:64])
                pe.transpose(bank[4][0:S, 256:320], dtp[:, SEQ:T], ident[0:64, 0:64]).then_inc(dt_turned, 1)

            def decays(p, first):
                pe.wait_ge(conv_done, 2 * (2 * GROUPS + p) + 2)
                if not first:
                    pe.wait_ge(hT_ready, p)
                if not first:
                    pe.wait_ge(y_step, 5 * p)
                for c in range(NC):
                    pe.transpose(bank[5][:, c * L:(c + 1) * L], xs[:, c * L:(c + 1) * L], ident)
                pe.transpose(bank[7][0:S, 0:P], xs[:, SEQ:T], ident).then_inc(x_turned, 1)
                pe.wait_ge(seg_lhs, 3 * p + 3)
                if not first:
                    pe.wait_ge(h_step, 4 * p)
                if not first:
                    pe.wait_ge(ss_final, p)
                for h in range(2):
                    for c in range(NC):
                        pe.matmul(bank[2 + h][:, c * L:(c + 1) * L], segL[:, h, c, :], tri, start=True, stop=True)
                    pe.matmul(bank[6][0:S, 72 * h:72 * h + S + 1], segLs[:, h, :], tri_s, start=True, stop=True)
                for c in range(NC):
                    pe.matmul(bank[4][:, c * L:(c + 1) * L],
                              pairA[:, c, :, :], tri, start=True, stop=True)
                pe.matmul(bank[6][:, 144:144 + S], pairA[0:S, NC, :, :],
                          tri_s[:, 0:S], start=True, stop=True).then_inc(seg_ready, 1)

            def states(p, g):
                pe.wait_ge(decay_ready, 5 * p + 5)
                pe.wait_ge(xdd_ready, 2 * p + 2)
                for c in range(NC):
                    last = pe.matmul(bank[2][:, c * P:(c + 1) * P], xdd[:, c, :], Btm[:, g, c, :], start=True, stop=True)
                last.then_inc(s_ready, 1)
                pe.wait_ge(bm_ready, g + 1)
                for b in range(2):
                    last = pe.matmul(bank[3 + b][:, :], xdd[0:S, NC, :], Bm[:, 4 * b:4 * b + 4, :], start=True, stop=True)
                last.then_inc(ss_ready, 1)

            def turn_states(p):
                pe.wait_ge(h_step, 4 * p + 3)
                pe.wait_ge(xdt_ready, 2 * p + 2)
                for c in range(NC - 1):
                    last = pe.transpose(bank[5][:, c * P:(c + 1) * P], hst[:, c, :], ident)
                last.then_inc(h_turned, 1)

            def outputs(p, g):
                pe.wait_ge(hT_ready, p + 1)
                pe.wait_ge(m_ready, p + 1)
                pe.wait_ge(h0t_loaded, 16 * p + 16)
                for c in range(1, NC):
                    pe.matmul(bank[6][:, (c - 1) * L:c * L], hT[:, c - 1, :], CT[:, g, c * L:(c + 1) * L],
                              start=True, stop=True)
                for b in range(DEC_BATCH):
                    at = SEQ + b * DEC_SEQ
                    pe.matmul(bank[6][:, at - L:at - L + DEC_SEQ], h0T[:, b, :], CT[:, g, at:at + DEC_SEQ],
                              start=True, stop=True)
                for h in range(2):
                    rows = slice(h * HEAD_DIM, (h + 1) * HEAD_DIM)
                    pe.matmul(bank[6][rows, 448:512], xdt[0:S, NC, rows], E[0:S, h, SEQ:T], start=True, stop=True)
                    for c in range(NC):
                        cols = slice(c * L, (c + 1) * L)
                        last = pe.matmul(bank[7][rows, cols], xdt[:, c, rows], E[:, h, cols], start=True, stop=True)
                last.then_inc(ssd_done, 1)

            def heads():
                n, m = PLAN["xz"], TILE["xz"]

                def body(p, g, first=False, project=True, stats=None):
                    j = p + 1
                    if project:
                        pe.wait_ge(evicted, m + 2 * j + 2)
                        half_unit(n, 2 * j, 0, 0)
                    decays(p, first)
                    if project:
                        half_unit(n, 2 * j, 0, 1)
                    states(p, g)
                    if project:
                        pe.wait_ge(evicted, m + 2 * j + 3)
                        if stats is not None:
                            group_sum(stats, 0)
                            pe.wait_ge(gvar, stats + 1)
                        half_unit(n + 1, 2 * j, 0, 0)
                    turn_states(p)
                    if project:
                        half_unit(n + 1, 2 * j, 0, 1)
                    outputs(p, g)

                pe.wait_ge(evicted, m)
                half_unit(n, 0, 1, 0)
                half_unit(n, 0, 1, 1)
                b_c_products()
                turn_dt()
                pe.wait_ge(evicted, m + 3)
                half_unit(n + 1, 0, 0, 0)
                half_unit(n + 1, 0, 0, 1)
                pe.wait_ge(dt_kept, 2)
                body(0, 0, first=True)
                with pe.Fori(1, 4) as p:
                    body(p, 0)
                with pe.Fori(1, GROUPS - 1) as g:
                    with pe.Fori(0, 4) as q:
                        body(g * 4 + q, g)
                with pe.Fori(0, GROUPS - 1) as q:
                    body(q + 12, GROUPS - 1, stats=q)
                body(NX - 1, GROUPS - 1, project=False)

            def group_sum(g, b):
                if b == 6:
                    pe.wait_ge(y_step, 5 * NX)
                pe.wait_ge(gsum_step, 4 * g + 4)
                for half in range(2):
                    last = pe.matmul(psum[:, b + half, 0:HALF], cst[:, C_ONES:C_ONES + P],
                                     gsum[:, g, half * HALF:(half + 1) * HALF], start=True, stop=True)
                last.then_inc(gnorm_sum, 1)

            def mixer_out():
                pe.wait_ge(evicted, TILE["out"] + 2)
                residual("out", [NK, NK], yhi, ylo, y_lo, 0, kwise=True)

            def turn_keys_values():
                for c in range(2):
                    for b in range(NC):
                        pe.transpose(psum[:, 2 + b // 2, (b % 2) * 256 + c * P:(b % 2) * 256 + (c + 1) * P],
                                     KVT[:, 2 + c, b * L:(b + 1) * L], ident)
                    pe.transpose(bank[6][:, c * P:(c + 1) * P], KVT[:, c, SEQ - L:SEQ], ident)
                for c in range(4):
                    last = pe.transpose(bank[7][0:S, c * P:(c + 1) * P], KVT[:, c, SEQ:T], ident)
                last.then_inc(kv_turned, 1)

            def scores(j, kp):
                pe.wait_ge(evicted, TILE["q"] + j + 3)
                for h in range(2):
                    rows = slice(HD * h, HD * (h + 1))
                    if h == 1:
                        pe.wait_ge(pt_ready, 2 * j)
                    for c in range(NC):
                        at = 2 * L * c
                        keys = slice(max(c - 1, 0) * L, (c + 1) * L)
                        lo_col = at if c else L
                        last = pe.matmul(psum[:, 2 + 2 * h + lo_col // 512, lo_col % 512:lo_col % 512 + (keys.stop - keys.start)],
                                         qs[rows, c * L:(c + 1) * L], KVT[rows, kp, keys], start=True, stop=True)
                    last.then_inc(scores_done, 1)

            def turn_probs(j):
                for h in range(2):
                    pe.wait_ge(p_ready, 2 * j + h + 1)
                    if h == 0:
                        pe.wait_ge(o_lo, j)
                    for t in range(2 * NC - 1):
                        last = pe.transpose(psum[:, (6 if h == 0 else 4) + t // 4, (t % 4) * P:(t % 4 + 1) * P],
                                            probs[:, h, (t + 1) * P:(t + 2) * P], ident)
                    last.then_inc(p_turned, 1)

            def weigh_values(j, kp):
                pe.wait_ge(pt_ready, 2 * j + 2)
                for h in range(2):
                    v = slice((2 * kp + h) * HD, (2 * kp + h + 1) * HD)
                    for c in range(NC):
                        out = bank[6][HD * h:HD * (h + 1), c * L:(c + 1) * L]
                        if c:
                            pe.matmul(out, VT[:, c - 1, v], PT[:, h, 2 * c - 1, :], start=True, stop=False)
                        last = pe.matmul(out, VT[:, c, v], PT[:, h, 2 * c, :], start=c == 0, stop=True)
                last.then_inc(pv_done, 1)

            def attention():
                n, m = PLAN["q"], TILE["q"]

                def body(g, kp, first=False):
                    j = 2 * g + kp
                    pe.wait_ge(evicted, m + j + (1 if first else 2))
                    unit(n + kp, 2 * g, NK, 0, xhi, xlo, 0, True, True, (xg_lo, NK * XG["q"]) if first else None,
                         norm_after=NORM["q"] if first else None)
                    if first:
                        turn_keys_values()
                        pe.wait_ge(kv_kept, 3)
                    else:
                        turn_probs(j - 1)
                    scores(j, kp)
                    if not first:
                        weigh_values(j - 1, 1 - kp)

                body(0, 0, first=True)
                body(0, 1)
                with pe.Fori(1, QH // KVH) as g:
                    body(g, 0)
                    body(g, 1)
                sample_scores()
                turn_probs(NK - 1)
                weigh_values(NK - 1, 1)

            def sample_scores():
                pe.wait_ge(soft, 4 * (2 * NK - 2) + 2)
                pe.wait_ge(qsam_ready, NK * 2)
                pe.wait_ge(ksam_ready, KVH)
                pe.wait_ge(kcache_loaded, 16)
                for b in range(DEC_BATCH):
                    for kv in range(KVH):
                        last = pe.matmul(psum[32 * kv:32 * kv + 32, b // 3, (b % 3) * KS:(b % 3 + 1) * KS],
                                         Qsam[:, kv, b, :, :].rearrange("p g t -> p (g t)"), Ksam[:, kv, b, :],
                                         start=True, stop=True)
                last.then_inc(ssc_done, 1)

            def sample_attention():
                pe.wait_ge(sp_ready, 1)
                pe.wait_ge(o_lo, NK)
                for b in range(DEC_BATCH):
                    pe.transpose(psum[:, 5 + b // 4, (b % 4) * P:(b % 4 + 1) * P], psam[:, b, 0:WINDOW], ident)
                for b in range(DEC_BATCH):
                    last = pe.transpose(psum[0:DEC_SEQ, (7, 2)[b // 4], (b % 4) * P:(b % 4 + 1) * P],
                                        psam[:, b, WINDOW:KS], ident)
                last.then_inc(sp_turned, 1)
                pe.wait_ge(spt_ready, 3)
                pe.wait_ge(vsam_loaded, 16)
                pe.wait_ge(vnew_loaded, 16)
                for b in range(DEC_BATCH):
                    for kv in range(KVH):
                        out = bank[3][HD * (kv % 2):HD * (kv % 2 + 1), (kv // 2) * 256 + b * 32:(kv // 2) * 256 + (b + 1) * 32]
                        v = slice(kv * HD, (kv + 1) * HD)
                        pe.matmul(out, Vsam[:, b, v], PTs[:, b, 32 * kv:32 * kv + 32], start=True, stop=False)
                        last = pe.matmul(out, Vnew[:, b, v], PTn[:, b, 32 * kv:32 * kv + 32], start=False, stop=True)
                last.then_inc(spv_done, 1)

            gate_up("gu0")
            residual("down0", down_widths(NF), hhi, hlo, h_lo, 0)
            b_and_c()
            heads()
            mixer_out()
            gate_up("gu1")
            residual("down1", down_widths(NF), hhi, hlo, h_lo, NF)
            key_value()
            gate_up("gu2", with_norm=False)
            residual("down2", down_widths(NF), hhi, hlo, h_lo, 2 * NF)
            attention()
            sample_attention()
            pe.wait_ge(evicted, TILE["o"] + 2)
            residual("o", [NK], ohi, olo, o_lo, 2)
            gate_up("gu3")
            residual("down3", down_widths(NF), hhi, hlo, h_lo, 3 * NF)
            norm(NORM["final"])

        @block.scalar
        def _(act):
            act.dma_start(prm[:], params).then_inc(prm_loaded, 16)
            act.dma_start(cst[:], consts).then_inc(c_loaded, 16)

            def split_hi(n, step):
                act.wait_ge(raw_loaded[n % 2], 16 * (n // 2 + 1) + 8 * step)
                if n >= 2:
                    act.wait_ge(units_done, n + step - 1)
                act.activation(whi[n % 2][:], wraw[n % 2][:], ACT.Copy).then_inc(weights_hi, 1)

            def gained(k, gain):
                act.activation(xhi[:, k, :], x[:, k, :], ACT.Copy, scale=prm[:, gain + k:gain + k + 1] if isinstance(k, int)
                               else prm[:, bass.ds(k + gain, 1)]).then_inc(xg_hi, 1)

            def std(e):
                act.wait_ge(var_ready, e + 1)
                act.activation(rstd[:], rstd[:], ACT.Sqrt).then_inc(std_ready, 1)

            def gate_up(ph, before, with_norm=True):
                n, m = PLAN[ph], TILE[ph]

                def body(i, first=False):
                    if first and with_norm:
                        std(NORM[ph])
                    split_hi(n + 2, 2 * i)
                    act.wait_ge(evicted, m + 2 * i + 3)
                    act.wait_ge(h_ready, NF * before + i)
                    act.activation(silu[:], gate[:], ACT.Silu).then_inc(silu_ready, 1)
                    split_hi(n + 3, 2 * i)
                    act.wait_ge(h_ready, NF * before + i + 1)
                    act.activation(hhi[:, i, :], hidden[:], ACT.Copy).then_inc(h_hi, 1)
                body(0, True)
                with act.Fori(1, NF) as i:
                    body(i)

            def residual(ph, per, gain, last=False):
                n, m = PLAN[ph], TILE[ph]

                def body(i, splits=2 * per):
                    for d in range(2):
                        for a in range(per):
                            if per * d + a < splits:
                                split_hi(n + 2 + per * d + a, 2 * per * i)
                        if gain is not None:
                            act.wait_ge(evicted, m + 2 * i + d + 3)
                            gained(2 * i + d, gain)
                with act.Fori(0, NK // 2 - 1) as i:
                    body(i)
                body(NK // 2 - 1, 2 * per - 2 if last else 2 * per)


            def conv_act(c):
                act.wait_ge(conv_step, 4 * c + 4)
                act.activation(th[:, 0:CLEN], cacc[:, 0:CLEN], ACT.Tanh).then_inc(conv_tanh, 1)

            def b_and_c():
                n = PLAN["bc"]
                std(NORM["dt"])
                split_hi(PLAN["dt"] + 2, 0)
                for c in range(2 * GROUPS):
                    split_hi(n + c + 2, 0)
                    act.wait_ge(evicted, TILE["bc"] + c + 3)
                    if c:
                        act.wait_ge(conv_done, 2 * c)
                    act.activation(cacc[:, 0:CLEN], cbuf[:, 0:CLEN], ACT.Identity, scale=column(G_CONVW, NX + c, CONV),
                                   bias=column(G_CONVB, NX + c)).then_inc(conv_step, 1)
                    conv_act(c)
                    if c in (0, 2):
                        softplus(c // 2)

            def softplus(part):
                s1, e, u, ln, r = dts
                if part == 0:
                    act.wait_ge(st_loaded, 32)
                    act.wait_ge(evicted, TILE["dt"] + 3)
                    act.activation(e[:], s1[:], ACT.Abs, bias=dtprm[:, 0:1]).then_inc(dt_act, 1)
                    act.activation(dtprm[:, 2:3], dtprm[:, 1:2], ACT.Exp).then_inc(dt_act, 1)
                    act.wait_ge(dt_act, 1)
                    act.activation(e[:], e[:], ACT.Exp, scale=-1.0).then_inc(dt_act, 1)
                else:
                    act.wait_ge(dt_dve, 2)
                    act.activation(ln[:], u[:], ACT.Ln).then_inc(dt_act, 1)
                    act.wait_ge(dt_act, 4)
                    act.activation(r[:], ln[:], ACT.Exp, scale=-1.0).then_inc(dt_act, 1)

            def keep_b():
                for g in range(GROUPS):
                    b = 2 + 3 * (g % 2)
                    act.wait_ge(b_turned, g + 1)
                    act.activation(Btm[:, g, 0:NC, :], bank[b][:, :].rearrange("p (c n) -> p c n", c=NC),
                                   ACT.Copy).then_inc(b_kept, 1)
                    act.activation(Btm[0:S, g, NC, :], bank[b + 1][0:S, 0:P], ACT.Copy).then_inc(b_kept, 1)

            def exponentials(p, first):
                act.wait_ge(seg_ready, p + 1)
                if not first:
                    act.wait_ge(ssd_done, p)
                if not first:
                    act.wait_ge(y_step, 5 * p)
                for h in range(2):
                    act.activation(E[:, h, 0:SEQ], bank[2 + h][:, :], ACT.Exp).then_inc(decay_ready, 1)
                act.activation(E[0:S, :, SEQ:T + 1],
                               bank[6][0:S, 0:144].rearrange("p (h t) -> p h t", h=2)[:, :, 0:S + 1],
                               ACT.Exp).then_inc(decay_ready, 1)
                act.activation(E2[:, 0:SEQ], bank[4][:, :], ACT.Exp).then_inc(decay_ready, 1)
                act.activation(E2[:, SEQ:T], bank[6][:, 144:144 + S], ACT.Exp).then_inc(decay_ready, 1)

            def heads():
                n = PLAN["xz"]

                def z_act(j):
                    act.wait_ge(evicted, TILE["xz"] + 2 * j + 4)
                    act.wait_ge(conv_done, 2 * (j + 2 * GROUPS) + 2)
                    act.activation(th[:, 0:T], yall[:, j, :], ACT.Tanh).then_inc(z_tanh, 1)

                def body(p, first=False, project=True, stats=None):
                    j = p + 1
                    exponentials(p, first)
                    if project:
                        split_hi(n + 2, 2 * j)
                    if stats is not None:
                        group_std(stats)
                    act.wait_ge(h_turned, p + 1)
                    act.activation(hT[:], bank[5][:, 0:(NC - 1) * P].rearrange("p (c n) -> p c n", c=NC - 1),
                                   ACT.Copy).then_inc(hT_ready, 1)
                    if project:
                        act.wait_ge(z_ready, j)
                        conv_act(j + 2 * GROUPS)
                        split_hi(n + 3, 2 * j)
                        z_act(j)

                split_hi(n + 2, 0)
                keep_b()
                conv_act(2 * GROUPS)
                split_hi(n + 3, 0)
                z_act(0)
                body(0, first=True)
                with act.Fori(1, NX - GROUPS) as p:
                    body(p)
                with act.Fori(0, GROUPS - 1) as q:
                    body(q + 12, stats=q)
                body(NX - 1, project=False)

            def group_std(g):
                act.wait_ge(gvar, g + 1)
                act.activation(gsum[:, g, :], gsum[:, g, :], ACT.Sqrt).then_inc(gstd, 1)

            def mixer_out(gain):
                act.wait_ge(ssd_done, NX)
                for p in range(NX):
                    if p == 8:
                        group_std(GROUPS - 1)
                    act.wait_ge(yn_ready, p + 1)
                    act.activation(yhi[:, p, :], yall[:, p, :], ACT.Copy, scale=column(G_GATE, p)).then_inc(y_hi, 1)
                residual("out", 2, gain)

            def key_value(gain):
                n = PLAN["kv"]
                std(NORM["kv"])
                for c in range(4):
                    split_hi(n + c + 2, 0)
                for k in range(NK):
                    if k < NK - 1:
                        act.wait_ge(xg_used, k + 1)
                    else:
                        act.wait_ge(units_done, n + 4)
                    gained(k, gain)

            def attention():
                n, m = PLAN["q"], TILE["q"]

                def copy_probs(j):
                    for h in range(2):
                        b = 6 if h == 0 else 4
                        act.wait_ge(p_turned, 2 * j + h + 1)
                        act.wait_ge(pv_done, j)
                        act.activation(PT[:, h, :, :].rearrange("p t q -> p (t q)"),
                                       psum[:, b:b + 2, :].rearrange("p b n -> p (b n)")[:, 0:(2 * NC - 1) * P],
                                       ACT.Copy).then_inc(pt_ready, 1)

                def exponentials(g, kp):
                    for h in range(2):
                        hh = 4 * g + 2 * kp + h
                        act.wait_ge(soft, 4 * hh + 4)
                        for c in range(NC):
                            act.activation(probs[:, h, 2 * L * c:2 * L * (c + 1)], sc[:, h, 2 * L * c:2 * L * (c + 1)],
                                           ACT.Exp, bias=nmax[:, h, c:c + 1],
                                           accum_out=rsum[:, h, c:c + 1]).then_inc(p_exp, 1)
                        head = g + 8 * kp + 4 * h
                        act.activation(esink[:, h, :], nmax[:, h, :], ACT.Exp,
                                       bias=acol(SINK, head)).then_inc(p_exp, 1)

                def out_hi(j):
                    act.wait_ge(pv_done, j + 1)
                    act.activation(ohi[:, j, 0:SEQ], bank[6][:, :], ACT.Copy).then_inc(o_hi, 1)

                def body(g, kp, first=False):
                    j = 2 * g + kp
                    if first:
                        std(NORM["q"])
                    split_hi(n + 2 + kp, 2 * g)
                    if first:
                        act.wait_ge(kv_turned, 1)
                        act.activation(VT[:].rearrange("p b v -> p (b v)").rearrange("p (a n) -> p a n", a=2), psum[:, 2:4, :],
                                       ACT.Copy).then_inc(kv_kept, 1)
                        act.activation(Kwin[:], bank[6][:, 0:2 * P], ACT.Copy).then_inc(kv_kept, 1)
                        act.activation(kvsam[:], bank[7][0:S, :], ACT.Copy).then_inc(kv_kept, 1)
                    act.wait_ge(evicted, m + j + 3)
                    for h in range(2):
                        act.activation(Qsam[:, 2 * kp + h, :, g, :],
                                       qs[HD * h:HD * (h + 1), SEQ:T].rearrange("p (b t) -> p b t", b=DEC_BATCH),
                                       ACT.Copy).then_inc(qsam_ready, 1)
                    if not first:
                        copy_probs(j - 1)
                    exponentials(g, kp)
                    if not first:
                        out_hi(j - 1)

                body(0, 0, first=True)
                body(0, 1)
                with act.Fori(1, QH // KVH) as g:
                    body(g, 0)
                    body(g, 1)
                copy_probs(NK - 1)
                sample_exponentials()
                out_hi(NK - 1)

            def sample_exponentials():
                act.wait_ge(ssoft, 5)
                for b in range(DEC_BATCH):
                    act.activation(psam[:, b, :], ssam[:, b, :], ACT.Exp, bias=snmax[:, b:b + 1],
                                   accum_out=srsum[:, b:b + 1]).then_inc(sp_exp, 1)
                act.activation(sesink[:], snmax[:], ACT.Exp, bias=acol(SINK_S, 0)).then_inc(sp_exp, 1)

            def sample_attention():
                act.wait_ge(sp_turned, 1)
                act.activation(PTs[:].rearrange("p b r -> p (b r)").rearrange("p (a n) -> p a n", a=2), psum[:, 5:7, :],
                               ACT.Copy).then_inc(spt_ready, 1)
                for i, b in enumerate((7, 2)):
                    act.activation(PTn[:, 4 * i:4 * i + 4, :].rearrange("p b r -> p (b r)"), bank[b][0:DEC_SEQ, :],
                                   ACT.Copy).then_inc(spt_ready, 1)
                act.wait_ge(spv_done, 1)
                for kp in range(2):
                    act.activation(ohi[:, kp:NK:2, SEQ:T].rearrange("p g (b t) -> p g b t", b=DEC_BATCH),
                                   bank[3][:, 256 * kp:256 * kp + 256].rearrange("p (b g t) -> p g b t", b=DEC_BATCH, g=4),
                                   ACT.Copy).then_inc(o_hi, 1)

            act.wait_ge(prm_loaded, 16)
            split_hi(0, 0)
            for k in range(NK):
                act.wait_ge(x_loaded[k], 16)
                gained(k, G_FFN1)
                if k == 0:
                    act.activation(sqsum[:], x[:, 0, :], ACT.Square).then_inc(sumsq, 1)
                else:
                    act.activation(firstsq[:, k - 1, :], x[:, k, :], ACT.Square).then_inc(squared, 1)
                if k == 1:
                    split_hi(1, 0)
            gate_up("gu0", 0)
            residual("down0", 3, G_MIX)
            b_and_c()
            heads()
            mixer_out(G_FFN2)
            gate_up("gu1", 1)
            residual("down1", 3, G_KV)
            key_value(G_FFN1 + NK)
            gate_up("gu2", 2, with_norm=False)
            residual("down2", 3, G_MIX + NK)
            attention()
            sample_attention()
            residual("o", 1, G_FFN2 + NK)
            gate_up("gu3", 3)
            residual("down3", 3, None, last=True)
            std(NORM["final"])

        @block.vector
        def _(dve):
            dve.sem_inc(evicted, 2)

            def split_lo(n, step):
                dve.wait_ge(weights_hi, n + step + 1)
                dve.tensor_tensor(wlo[n % 2][:], wraw[n % 2][:], whi[n % 2][:].bitcast(F32),
                                  ALU.subtract).then_inc(weights_lo, 1)

            def gained_lo(k, gain, q):
                dve.wait_ge(xg_hi, NK * q + k + 1)
                g = prm[:, gain + k:gain + k + 1] if isinstance(k, int) else prm[:, bass.ds(k + gain, 1)]
                dve.scalar_tensor_tensor(xlo[:, k, :], x[:, k, :], g, xhi[:, k, :].bitcast(F32),
                                         ALU.mult, ALU.subtract).then_inc(xg_lo, 1)

            def rms(e):
                dve.wait_ge(norm_sum, e + 1)
                dve.tensor_scalar(halves(rstd[:]), nrm[:, :, 0:HALF], 1.0 / D_MODEL, EPS, ALU.mult,
                                  ALU.add).then_inc(var_ready, 1)
                dve.wait_ge(std_ready, e + 1)
                dve.reciprocal(rstd[:], rstd[:]).then_inc(rstd_ready, 1)
                dve.wait_ge(rstd_ready, e + 1)

            def hidden_lo(before, i):
                dve.wait_ge(h_hi, NF * before + i + 1)
                dve.tensor_tensor(hlo[:, i, :], hidden[:], hhi[:, i, :].bitcast(F32),
                                  ALU.subtract).then_inc(h_lo, 1)

            def gate_up(ph, before, with_norm=True):
                n, m = PLAN[ph], TILE[ph]

                def body(i, first=False):
                    if first and with_norm:
                        rms(NORM[ph])
                    else:
                        split_lo(n + 2, 2 * i)
                    dve.wait_ge(units_done, n + 2 * i + 1)
                    if before or not first:
                        dve.wait_ge(silu_ready, NF * before + i)
                    dve.tensor_tensor(halves(gate[:]), out_of(m % 2), halves(rstd[:]), ALU.mult).then_inc(evicted, 1)
                    if first and with_norm:
                        split_lo(n + 2, 2 * i)
                    if not first:
                        hidden_lo(before, i - 1)
                    split_lo(n + 3, 2 * i)
                    dve.wait_ge(units_done, n + 2 * i + 2)
                    dve.tensor_tensor(halves(up[:]), out_of((m + 1) % 2), halves(rstd[:]), ALU.mult).then_inc(evicted, 1)
                    dve.wait_ge(silu_ready, NF * before + i + 1)
                    dve.wait_ge(evicted, m + 2 * i + 4)
                    dve.tensor_tensor(hidden[:], silu[:], up[:], ALU.mult).then_inc(h_ready, 1)
                body(0, True)
                with dve.Fori(1, NF) as i:
                    body(i)
                hidden_lo(before, NF - 1)

            def residual(ph, per, gain, q, scale=None, last=False, kwise=False):
                n, m = PLAN[ph], TILE[ph]

                def body(i, first=False, splits=2 * per):
                    for d in range(2):
                        for a in range(per):
                            if per * d + a < splits:
                                split_lo(n + 2 + per * d + a, 2 * per * i)
                            if a == 0 and not (first and d == 0) and gain is not None:
                                gained_lo(2 * i + d - 1, gain, q)
                        dve.wait_ge(units_done, n + 2 * per - 1 + d if first and kwise
                                    else n + 2 * per * i + per * d + per)
                        tile = halves(x[:, 2 * i + d, :])
                        if scale is None:
                            dve.tensor_tensor(tile, out_of((m + d) % 2), tile, ALU.add).then_inc(evicted, 1)
                        else:
                            dve.scalar_tensor_tensor(tile, out_of((m + d) % 2), scale, tile, ALU.mult,
                                                     ALU.add).then_inc(evicted, 1)
                body(0, True)
                with dve.Fori(1, NK // 2 - 1) as i:
                    body(i)
                body(NK // 2 - 1, splits=2 * per - 2 if last else 2 * per)
                if gain is not None:
                    gained_lo(NK - 1, gain, q)


            def seq_rows(buf):
                return buf[:, 3 + SEQ:CBUF].rearrange("p (b r) -> p b r", b=DEC_BATCH)[:, :, 0:DEC_SEQ]

            def conv_in(c, ci, pair, last_inc=evicted):
                dve.wait_ge(conv_saved, 2 * ci)
                seqs = cbuf[:, 3 + SEQ:CBUF].rearrange("p (b r) -> p b r", b=DEC_BATCH)
                dve.tensor_copy(seqs[:, :, 0:3], cstate[:, c, :, :])
                dve.tensor_tensor(cbuf[:, 3:3 + HALF], acc[:, 2 * pair, 0:HALF], rstd[:, 0:HALF], ALU.mult)
                dve.tensor_tensor(cbuf[:, 3 + HALF:3 + SEQ], acc[:, 2 * pair + 1, 0:SEQ - HALF], rstd[:, HALF:SEQ],
                                  ALU.mult)
                dve.tensor_tensor(seqs[:, :, 3:3 + DEC_SEQ],
                                  acc[:, 2 * pair + 1, SEQ - HALF:HALF].rearrange("p (b t) -> p b t", b=DEC_BATCH),
                                  rstd[:, SEQ:T].rearrange("p (b t) -> p b t", b=DEC_BATCH), ALU.mult).then_inc(evicted, 1)

            def conv_taps(c, ci, tile, on_act=False):
                dve.wait_ge(evicted, tile + 3)
                if not on_act:
                    dve.tensor_scalar(cacc[:, 0:CLEN], cbuf[:, 0:CLEN], column(G_CONVW, c, CONV), column(G_CONVB, c), ALU.mult,
                                      ALU.add).then_inc(conv_step, 1)
                for tap in range(1, CONV):
                    dve.wait_ge(conv_step, 4 * ci + tap)
                    dve.scalar_tensor_tensor(cacc[:, 0:CLEN], cbuf[:, tap:tap + CLEN], column(G_CONVW + tap, c, CONV), cacc[:, 0:CLEN],
                                             ALU.mult, ALU.add).then_inc(conv_step, 1)

            def conv_out(out, ci):
                dve.wait_ge(conv_tanh, ci + 1)
                dve.scalar_tensor_tensor(out[:, 0:SEQ], th[:, 0:SEQ], 1.0, cacc[:, 0:SEQ], ALU.add,
                                         ALU.mult).then_inc(conv_done, 1)
                dve.scalar_tensor_tensor(out[:, SEQ:T].rearrange("p (b t) -> p b t", b=DEC_BATCH), seq_rows(th), 1.0,
                                         seq_rows(cacc), ALU.add, ALU.mult).then_inc(conv_done, 1)

            def b_and_c():
                n, m = PLAN["bc"], TILE["bc"]
                rms(NORM["dt"])
                evict_dt()
                split_lo(PLAN["dt"] + 2, 0)
                for c in range(2 * GROUPS):
                    if c == 0:
                        split_lo(n + c + 2, 0)
                        dve.wait_ge(st_loaded, 32)
                        dve.wait_ge(cleared, 5)
                        dve.wait_ge(conv_prm, 1)
                    dve.wait_ge(units_done, n + c + 1)
                    conv_in(NX + c, c, (c + 1) % 2)
                    conv_taps(NX + c, c, m + c, on_act=True)
                    conv_out(BT[:, c, :] if c < GROUPS else CT[:, c - GROUPS, :], c)
                    if c in (1, 3):
                        softplus(c // 2)

            def evict_dt():
                dve.wait_ge(units_done, PLAN["dt"] + 1)
                dve.tensor_tensor(halves(dts[0][:]), psum[0:HEADS, 0:2, 0:HALF],
                                  halves(rstd[0:HEADS, :]), ALU.mult).then_inc(evicted, 1)

            def softplus(part):
                s1, e, u, ln, r = dts
                if part == 0:
                    dve.wait_ge(evicted, TILE["dt"] + 3)
                    dve.wait_ge(dt_act, 3)
                    dve.tensor_scalar(s1[:], s1[:], dtprm[:, 0:1], 0.0, ALU.add, ALU.max).then_inc(dt_dve, 1)
                    dve.tensor_scalar(u[:], e[:], 1.0, None, ALU.add).then_inc(dt_dve, 1)
                    dve.wait_ge(dt_dve, 2)
                    dve.scalar_tensor_tensor(e[:], u[:], -1.0, e[:], ALU.add, ALU.subtract).then_inc(dt_dve, 1)
                    return
                dve.wait_ge(dt_act, 5)
                dve.wait_ge(dt_dve, 3)
                dve.tensor_tensor(e[:], e[:], r[:], ALU.mult).then_inc(dt_dve, 1)
                dve.tensor_tensor(s1[:], s1[:], ln[:], ALU.add).then_inc(dt_dve, 1)
                dve.wait_ge(dt_dve, 5)
                dve.tensor_tensor(dtp[0:HEADS, :], s1[:], e[:], ALU.subtract).then_inc(dt_dve, 1)
                dve.wait_ge(dt_dve, 6)
                dve.tensor_scalar(dtp[HEADS:2 * HEADS, :], dtp[0:HEADS, :], dtprm[:, 2:3], -1.0, ALU.mult,
                                  ALU.mult).then_inc(dt_dve, 1)

            def keep_dt():
                dve.wait_ge(dt_turned, 1)
                dve.tensor_copy(dT[:, 0:NC, :], bank[4][:, 0:256].rearrange("p (c h) -> p c h", c=NC)).then_inc(dt_kept, 1)
                dve.tensor_copy(dT[0:S, NC, :], bank[4][0:S, 256:320]).then_inc(dt_kept, 1)
                dve.wait_ge(dt_kept, 2)

            def mask_cb():
                for g in range(GROUPS):
                    b = 2 + 3 * (g % 2)
                    dve.wait_ge(cb_done, g + 1)
                    dve.tensor_tensor(cbm[:, g, 0:SEQ].rearrange("p (c t) -> p c t", c=NC),
                                      bank[b + 2][:, :].rearrange("p (c t) -> p c t", c=NC),
                                      tri.unsqueeze(1).to_broadcast([P, NC, L]), ALU.mult).then_inc(cb_kept, 1)
                    dve.tensor_tensor(cbm[0:S, g, SEQ:T], bank[b + 1][0:S, P:P + S], tri_s[:, 0:S],
                                      ALU.mult).then_inc(cb_kept, 1)

            def heads():
                n, m = PLAN["xz"], TILE["xz"]

                def by_head(buf):
                    return buf.rearrange("p c (h d) -> p c h d", h=2)

                def weighted(p, first, finish):
                    dve.wait_ge(x_turned, p + 1)
                    if not first:
                        dve.wait_ge(ssd_done, p)
                    dt = dT[:, :, 0:HEADS].rearrange("p c (j h) -> p c j h", h=2)[:, :, p, :]
                    dve.tensor_tensor(by_head(xdt[:, 0:NC, :]), bank[5][:, :].rearrange("p (c h d) -> p c h d", c=NC, h=2),
                                      dt[:, 0:NC, :].unsqueeze(3).to_broadcast([P, NC, 2, HEAD_DIM]),
                                      ALU.mult).then_inc(xdt_ready, 1)
                    dve.tensor_tensor(xdt[0:S, NC, :].rearrange("p (h d) -> p h d", h=2),
                                      bank[7][0:S, 0:P].rearrange("p (h d) -> p h d", h=2),
                                      dt[0:S, NC, :].unsqueeze(2).to_broadcast([S, 2, HEAD_DIM]),
                                      ALU.mult).then_inc(xdt_ready, 1)
                    if finish is not None:
                        group_rstd(finish)
                    dve.wait_ge(decay_ready, 5 * p + 3)
                    dve.wait_ge(xdt_ready, 2 * p + 2)
                    to_end = E[:, :, L - 1:SEQ:L].rearrange("p h c -> p c h")
                    dve.tensor_tensor(by_head(xdd[:, 0:NC, :]), by_head(xdt[:, 0:NC, :]),
                                      to_end.unsqueeze(3).to_broadcast([P, NC, 2, HEAD_DIM]), ALU.mult).then_inc(xdd_ready, 1)
                    dve.tensor_tensor(xdd[0:S, NC, :].rearrange("p (h d) -> p h d", h=2),
                                      xdt[0:S, NC, :].rearrange("p (h d) -> p h d", h=2),
                                      E[0:S, :, T:T + 1].to_broadcast([S, 2, HEAD_DIM]), ALU.mult).then_inc(xdd_ready, 1)

                def chain(p, first):
                    dve.wait_ge(s_ready, p + 1)
                    if not first:
                        dve.wait_ge(hp_stored, 16 * p)
                    dve.tensor_copy(hst[:, 0, :], bank[2][:, 0:P]).then_inc(h_step, 1)
                    for c in range(1, NC):
                        dve.wait_ge(h_step, 4 * p + c)
                        dve.scalar_tensor_tensor(hst[:, c, :], hst[:, c - 1, :], E2[:, c * L + L - 1:c * L + L],
                                                 bank[2][:, c * P:(c + 1) * P], ALU.mult, ALU.add).then_inc(h_step, 1)

                def gated(p):
                    dve.wait_ge(ssd_done, p + 1)
                    dve.wait_ge(skip_ready, p + 1)
                    dve.tensor_tensor(yd[:, 0:SEQ], yd[:, 0:SEQ], bank[7][:, :], ALU.add).then_inc(y_step, 1)
                    dve.tensor_tensor(yd[:, SEQ:T], yd[:, SEQ:T], bank[6][:, 448:512], ALU.add).then_inc(y_step, 1)
                    dve.tensor_tensor(yo[:, L:T], bank[6][:, 0:448], E2[:, L:T], ALU.mult).then_inc(y_step, 1)
                    dve.wait_ge(y_step, 5 * p + 3)
                    dve.tensor_tensor(yd[:, L:T], yd[:, L:T], yo[:, L:T], ALU.add).then_inc(y_step, 1)
                    dve.wait_ge(y_step, 5 * p + 4)
                    dve.wait_ge(z_ready, p + 1)
                    dve.tensor_tensor(yall[:, p, :], yd[:], yall[:, p, :], ALU.mult).then_inc(y_step, 1)

                def z_out(j):
                    dve.wait_ge(units_done, n + 2 * j + 2)
                    dve.scalar_tensor_tensor(halves(yall[:, j, :]), out_of(0), 0.5, halves(rstd[:]), ALU.mult,
                                             ALU.mult).then_inc(evicted, 1)

                def z_gate(j):
                    dve.wait_ge(z_tanh, j + 1)
                    dve.scalar_tensor_tensor(yall[:, j, :], th[:, 0:T], 1.0, yall[:, j, :], ALU.add,
                                             ALU.mult).then_inc(z_ready, 1)

                def body(p, g, first=False, project=True, stats=None, finish=None):
                    j = p + 1
                    weighted(p, first, finish)
                    if project:
                        dve.wait_ge(units_done, n + 2 * j + 1)
                        conv_in(j, j + 2 * GROUPS, 0)
                        split_lo(n + 2, 2 * j)
                    if stats is not None:
                        group_var(stats, 0)
                    dve.wait_ge(xdd_ready, 2 * p + 2)
                    dve.tensor_tensor(E[:, :, 0:T], E[:, :, 0:T], cbm[:, g, :].unsqueeze(1).to_broadcast([P, 2, T]),
                                      ALU.mult).then_inc(m_ready, 1)
                    chain(p, first)
                    if project:
                        conv_taps(j, j + 2 * GROUPS, m + 2 * j)
                    dve.wait_ge(ss_ready, p + 1)
                    dve.wait_ge(h0_decayed, p + 1)
                    dve.tensor_tensor(h0s[:].rearrange("p b n -> p (b n)").rearrange("p (a n) -> p a n", a=2), psum[:, 3:5, :],
                                      h0s[:].rearrange("p b n -> p (b n)").rearrange("p (a n) -> p a n", a=2),
                                      ALU.add).then_inc(ss_final, 1)
                    if project:
                        dve.wait_ge(x_turned, j)
                        dve.wait_ge(skip_ready, j)
                        conv_out(xs, j + 2 * GROUPS)
                        z_out(j)
                        split_lo(n + 3, 2 * j)
                    gated(p)
                    if project:
                        z_gate(j)

                dve.sem_inc(evicted, 1)
                dve.wait_ge(units_done, n + 1)
                conv_in(0, 2 * GROUPS, 1)
                mask_cb()
                conv_taps(0, 2 * GROUPS, m)
                dve.wait_ge(weights_lo, n + 2)
                split_lo(n + 2, 0)
                conv_out(xs, 2 * GROUPS)
                keep_dt()
                z_out(0)
                split_lo(n + 3, 0)
                z_gate(0)
                body(0, 0, first=True)
                with dve.Fori(1, 4) as p:
                    body(p, 0)
                with dve.Fori(1, GROUPS - 1) as g:
                    with dve.Fori(0, 4) as q:
                        body(g * 4 + q, g)
                body(12, GROUPS - 1, stats=0)
                with dve.Fori(1, GROUPS - 1) as q:
                    body(q + 12, GROUPS - 1, stats=q, finish=q - 1)
                body(NX - 1, GROUPS - 1, project=False, finish=GROUPS - 2)

            def group_var(g, b):
                dve.wait_ge(gnorm_sum, g + 1)
                dve.tensor_scalar(halves(gsum[:, g, :]), psum[:, b:b + 2, 0:HALF], float(GROUPS) / D_INNER, EPS,
                                  ALU.mult, ALU.add).then_inc(gvar, 1)

            def group_rstd(g):
                dve.wait_ge(gstd, g + 1)
                dve.reciprocal(gsum[:, g, :], gsum[:, g, :]).then_inc(grstd, 1)

            def group_norm(g):
                group_rstd(g)
                dve.wait_ge(grstd, g + 1)
                dve.wait_ge(yn_ready, 4 * g)
                for p in range(4 * g, 4 * g + 4):
                    dve.tensor_tensor(yall[:, p, :], yall[:, p, :], gsum[:, g, :], ALU.mult).then_inc(yn_ready, 1)

            def mixer_out(gain, q):
                for p in range(NX):
                    if p == 8:
                        group_var(GROUPS - 1, 6)
                        group_norm(GROUPS - 1)
                    low_part(p)
                residual("out", 2, gain, q, kwise=True)

            def low_part(p):
                dve.wait_ge(y_hi, p + 1)
                dve.scalar_tensor_tensor(ylo[:, p, :], yall[:, p, :], column(G_GATE, p), yhi[:, p, :].bitcast(F32),
                                         ALU.mult, ALU.subtract).then_inc(y_lo, 1)

            def key_value(gain, q):
                n, m = PLAN["kv"], TILE["kv"]
                rms(NORM["kv"])
                for c in range(4):
                    dve.wait_ge(units_done, n + c + 1)
                    dve.tensor_tensor(halves(KVT[:, c, :]), out_of((m + c) % 2), halves(rstd[:]), ALU.mult).then_inc(evicted, 1)
                    split_lo(n + c + 2, 0)
                for k in range(NK):
                    gained_lo(k, gain, q)

            def attention():
                n, m = PLAN["q"], TILE["q"]

                def softmax_in(g, kp):
                    for h in range(2):
                        hh = 4 * g + 2 * kp + h
                        head = g + 8 * kp + 4 * h
                        dve.wait_ge(scores_done, hh + 1)
                        flat = psum[:, 2 + 2 * h:4 + 2 * h, :].rearrange("p b n -> p (b n)")
                        by_block = lambda v: v.rearrange("p (c k) -> p c k", k=2 * L)
                        dve.scalar_tensor_tensor(by_block(sc[:, h, 2 * L:]),
                                                 negd[:].unsqueeze(1).to_broadcast([P, NC - 1, 2 * L]), acol(SLOPE, head),
                                                 by_block(flat[:, 2 * L:]), ALU.mult, ALU.add).then_inc(soft, 1)
                        dve.scalar_tensor_tensor(sc[:, h, L:2 * L], negd[:, L:2 * L], acol(SLOPE, head), flat[:, L:2 * L],
                                                 ALU.mult, ALU.add).then_inc(soft, 1)
                        dve.wait_ge(soft, 4 * hh + 2)
                        dve.tensor_reduce(nmax[:, h, :], by_block(sc[:, h, :]), mybir.AxisListType.X, ALU.max).then_inc(soft, 1)
                        dve.wait_ge(soft, 4 * hh + 3)
                        dve.tensor_scalar(nmax[:, h, :], nmax[:, h, :], acol(SINK, head), -1.0, ALU.max,
                                          ALU.mult).then_inc(soft, 1)

                def denominators(j):
                    for h in range(2):
                        hh = 2 * j + h
                        dve.wait_ge(p_exp, 5 * hh + 5)
                        dve.tensor_tensor(rsum[:, h, :], rsum[:, h, :], esink[:, h, :], ALU.add).then_inc(den, 1)
                        dve.wait_ge(den, 2 * hh + 1)
                        dve.wait_ge(p_ready, 2 * j)
                        dve.reciprocal(rden[:, h, :], rsum[:, h, :]).then_inc(den, 1)

                def out_lo(j):
                    dve.wait_ge(o_hi, j + 1)
                    dve.tensor_tensor(olo[:, j, 0:SEQ], bank[6][:, :], ohi[:, j, 0:SEQ].bitcast(F32),
                                      ALU.subtract).then_inc(o_lo, 1)

                def body(g, kp, first=False):
                    j = 2 * g + kp
                    if first:
                        rms(NORM["q"])
                    dve.wait_ge(units_done, n + j + 1)
                    if not first:
                        dve.wait_ge(scores_done, 2 * j)
                        dve.wait_ge(qsam_ready, 2 * j)
                    dve.scalar_tensor_tensor(halves(qs[:]), out_of(0), HD ** -0.5, halves(rstd[:]), ALU.mult,
                                             ALU.mult).then_inc(evicted, 1)
                    split_lo(n + 2 + kp, 2 * g)
                    softmax_in(g, kp)
                    denominators(j)
                    if not first:
                        out_lo(j - 1)

                dve.wait_ge(att_cleared, 1)
                dve.wait_ge(att_loaded, 16)
                body(0, 0, first=True)
                body(0, 1)
                with dve.Fori(1, QH // KVH) as g:
                    body(g, 0)
                    body(g, 1)
                sample_softmax()
                out_lo(NK - 1)

            def sample_softmax():
                dve.wait_ge(ssc_done, 1)
                for i, (b0, nb) in enumerate(((0, 3), (3, 3), (6, 2))):
                    dve.tensor_tensor(ssam[:, b0:b0 + nb, :], bank[i][:, 0:nb * KS].rearrange("p (b k) -> p b k", b=nb),
                                      attc[:, BIAS_S:BIAS_S + KS].unsqueeze(1).to_broadcast([P, nb, KS]),
                                      ALU.add).then_inc(ssoft, 1)
                dve.wait_ge(ssoft, 3)
                dve.tensor_reduce(snmax[:], ssam[:], mybir.AxisListType.X, ALU.max).then_inc(ssoft, 1)
                dve.wait_ge(ssoft, 4)
                dve.tensor_scalar(snmax[:], snmax[:], acol(SINK_S, 0), -1.0, ALU.max, ALU.mult).then_inc(ssoft, 1)
                dve.wait_ge(sp_exp, DEC_BATCH + 1)
                dve.tensor_tensor(srsum[:], srsum[:], sesink[:], ALU.add).then_inc(sden, 1)
                dve.wait_ge(sden, 1)
                dve.reciprocal(srden[:], srsum[:]).then_inc(sden, 1)
                dve.wait_ge(sden, 2)
                dve.tensor_tensor(psam[:], psam[:], srden[:].unsqueeze(2).to_broadcast([P, DEC_BATCH, KS]),
                                  ALU.mult).then_inc(sp_ready, 1)

            def sample_attention():
                for kp in range(2):
                    dve.wait_ge(o_hi, NK + kp + 1)
                    dve.wait_ge(o_hi, NK + 2)
                    dve.tensor_tensor(olo[:, kp:NK:2, SEQ:T].rearrange("p g (b t) -> p g b t", b=DEC_BATCH),
                                      bank[3][:, 256 * kp:256 * kp + 256].rearrange("p (b g t) -> p g b t", b=DEC_BATCH, g=4),
                                      ohi[:, kp:NK:2, SEQ:T].bitcast(F32).rearrange("p g (b t) -> p g b t", b=DEC_BATCH),
                                      ALU.subtract).then_inc(o_lo, 1)

            dve.wait_ge(prm_loaded, 16)
            conv_params = prm[:, G_CONVB:NPARAM]
            dve.tensor_scalar(conv_params, conv_params, 0.5, None, ALU.mult).then_inc(conv_prm, 1)
            split_lo(0, 0)
            for k in range(NK):
                gained_lo(k, G_FFN1, 0)
                if k == 1:
                    split_lo(1, 0)
            gate_up("gu0", 0)
            residual("down0", 3, G_MIX, 1, 0.5)
            b_and_c()
            heads()
            mixer_out(G_FFN2, 2)
            gate_up("gu1", 1)
            residual("down1", 3, G_KV, 3, 0.5)
            key_value(G_FFN1 + NK, 4)
            gate_up("gu2", 2, with_norm=False)
            residual("down2", 3, G_MIX + NK, 5, 0.5)
            attention()
            sample_attention()
            residual("o", 1, G_FFN2 + NK, 6)
            gate_up("gu3", 3)
            residual("down3", 3, None, None, 0.5, last=True)
            rms(NORM["final"])
            for k in range(NK):
                dve.scalar_tensor_tensor(ybuf[:, k, :], x[:, k, :], prm[:, G_FINAL + k:G_FINAL + k + 1], rstd[:],
                                         ALU.mult, ALU.mult).then_inc(y_ready, 1)

        @block.gpsimd
        def _(pool):
            def squares(e, first_tile):
                def body(k, first=False):
                    pool.wait_ge(evicted, first_tile + k + 3)
                    if first:
                        pool.tensor_tensor(sqsum[:], x[:, 0, :], x[:, 0, :], ALU.mult).then_inc(sumsq, 1)
                        return
                    pool.wait_ge(sumsq, NK * e + k)
                    pool.tensor_tensor(sq[:], x[:, k, :], x[:, k, :], ALU.mult).then_inc(squared, 1)
                    pool.wait_ge(squared, (NK - 1) * e + k)
                    pool.tensor_tensor(sqsum[:], sqsum[:], sq[:], ALU.add).then_inc(sumsq, 1)
                body(0, True)
                with pool.Fori(1, NK) as k:
                    body(k)

            def load_state(p):
                pool.dma_start(h0s[:], ssm_state[:, p, :, :].rearrange("b q n -> q b n")).then_inc(h0_loaded, 16)

            def load_state_t(p):
                pool.dma_start(h0T[:], ssm_state_t[:, p, :, :]).then_inc(h0t_loaded, 16)

            def prepare_mixer():
                pool.wait_ge(units_done, PLAN["bc"])
                pool.dma_start(cstate[:], conv_state).then_inc(st_loaded, 16)
                pool.dma_start(dtprm[:, 0:2], dt_params).then_inc(st_loaded, 16)
                load_state(0)
                load_state_t(0)
                pool.memset(cbuf[:, 0:3], 0.0).then_inc(cleared, 1)
                pool.memset(cbm[:, :, SEQ:T], 0.0).then_inc(cleared, 1)
                pool.memset(E[:, :, SEQ:T], 0.0).then_inc(cleared, 1)
                pool.memset(dT[:, NC, :], 0.0).then_inc(cleared, 1)
                pool.memset(gsum[:], 0.0).then_inc(cleared, 1)

            def keep_rows(c, ci, tile):
                pool.wait_ge(evicted, tile + 3)
                pool.tensor_copy(cnew[:, c, 0:3], cbuf[:, SEQ:SEQ + 3]).then_inc(conv_saved, 1)
                pool.tensor_copy(cstate[:, c, :, :],
                                 cbuf[:, 3 + SEQ:CBUF].rearrange("p (b r) -> p b r", b=DEC_BATCH)[:, :, DEC_SEQ:DEC_SEQ + 3]
                                 ).then_inc(conv_saved, 1)

            def seg_operands(p):
                dta = dT[:, :, HEADS:2 * HEADS].rearrange("p c (j h) -> p c j h", h=2)[:, :, p, :]
                pool.tensor_copy(pairA[:], dta.unsqueeze(3).to_broadcast([P, NC + 1, 2, HEAD_DIM])).then_inc(seg_lhs, 1)
                pool.tensor_tensor(segL[:].rearrange("p h c s -> p c h s"),
                                   strict.unsqueeze(1).unsqueeze(1).to_broadcast([P, NC, 2, L]),
                                   dta[:, 0:NC, :].unsqueeze(3).to_broadcast([P, NC, 2, L]), ALU.mult).then_inc(seg_lhs, 1)
                pool.tensor_tensor(segLs[:], strict_s.unsqueeze(1).to_broadcast([S, 2, S]),
                                   dta[0:S, NC, :].unsqueeze(2).to_broadcast([S, 2, S]), ALU.mult).then_inc(seg_lhs, 1)

            def heads():
                m = TILE["xz"]

                def body(p, g, first=False, more=True, finish=None):
                    pool.wait_ge(conv_done, 2 * (2 * GROUPS + p) + 2)
                    if not first:
                        pool.wait_ge(y_step, 5 * p)
                    pool.tensor_tensor(yd[:], xs[:], column(G_D, p).to_broadcast([P, T]), ALU.mult).then_inc(skip_ready, 1)
                    pool.wait_ge(decay_ready, 5 * p + 5)
                    pool.wait_ge(h0_loaded, 16 * p + 16)
                    pool.tensor_tensor(h0s[:], h0s[:],
                                       E2[:, SEQ + DEC_SEQ - 1:T:DEC_SEQ].unsqueeze(2).to_broadcast([P, DEC_BATCH, P]),
                                       ALU.mult).then_inc(h0_decayed, 1)
                    if more:
                        pool.wait_ge(seg_ready, p + 1)
                        seg_operands(p + 1)
                        keep_rows(p + 1, p + 1 + 2 * GROUPS, m + 2 * (p + 1))
                    pool.wait_ge(h_step, 4 * p + 4)
                    pool.wait_ge(h_turned, p + 1)
                    pool.wait_ge(ss_final, p + 1)
                    pool.dma_start(ssm_p_out[p], hst[:, NC - 1, :]).then_inc(hp_stored, 16)
                    pool.dma_start(ssm_s_out[:, p, :, :].rearrange("b q n -> q b n"), h0s[:]).then_inc(hs_stored, 16)
                    if more:
                        pool.wait_ge(hs_stored, 16 * p + 16)
                        load_state(p + 1)
                        pool.wait_ge(ssd_done, p + 1)
                        load_state_t(p + 1)
                    if finish is not None:
                        pool.wait_ge(grstd, finish + 1)
                        for i in range(4):
                            pool.tensor_tensor(yall[:, finish * 4 + i, :], yall[:, finish * 4 + i, :],
                                               gsum[:, finish, :], ALU.mult).then_inc(yn_ready, 1)
                    pool.wait_ge(y_step, 5 * p + 5)
                    if not first:
                        pool.wait_ge(gsum_step, p)
                    pool.tensor_tensor(sq[:], yall[:, p, :], yall[:, p, :], ALU.mult).then_inc(ysq, 1)
                    pool.wait_ge(ysq, p + 1)
                    pool.tensor_tensor(gsum[:, g, :], gsum[:, g, :], sq[:], ALU.add).then_inc(gsum_step, 1)

                def sequence_b(g, first=False):
                    if not first:
                        pool.wait_ge(ss_ready, 4 * g)
                    pool.tensor_tensor(Bm[:], Btm[0:S, g, NC, :].unsqueeze(1).to_broadcast([S, DEC_BATCH, P]),
                                       in_seq.unsqueeze(2).to_broadcast([S, DEC_BATCH, P]), ALU.mult).then_inc(bm_ready, 1)

                keep_rows(0, 2 * GROUPS, m)
                pool.wait_ge(dt_kept, 2)
                seg_operands(0)
                pool.wait_ge(b_kept, 2 * GROUPS)
                sequence_b(0, first=True)
                body(0, 0, first=True)
                with pool.Fori(1, 4) as p:
                    body(p, 0)
                with pool.Fori(1, GROUPS - 1) as g:
                    sequence_b(g)
                    with pool.Fori(0, 4) as q:
                        body(g * 4 + q, g)
                sequence_b(GROUPS - 1)
                body(12, GROUPS - 1)
                with pool.Fori(1, GROUPS - 1) as q:
                    body(q + 12, GROUPS - 1, finish=q - 1)
                body(NX - 1, GROUPS - 1, more=False, finish=GROUPS - 2)
                pool.wait_ge(conv_saved, 2 * NXBC)
                pool.dma_start(conv_p_out, cnew[:]).then_inc(cnew_stored, 16)
                pool.dma_start(conv_s_out, cstate[:]).then_inc(cnew_stored, 16)
                pool.wait_ge(cnew_stored, 32)
                pool.wait_ge(hp_stored, 16 * NX)
                pool.wait_ge(hs_stored, 16 * NX)

            def prepare_attention():
                pool.wait_ge(units_done, PLAN["q"])
                pool.dma_start(attc[:], att_consts).then_inc(att_loaded, 16)
                pool.memset(sc[:, :, 0:L], MASKED).then_inc(att_cleared, 1)
                pool.dma_start(Ksam[:, :, :, 0:WINDOW], cache_kt).then_inc(kcache_loaded, 16)
                pool.dma_start(Vsam[:], cache_v).then_inc(vsam_loaded, 16)

            def attention():
                pool.wait_ge(kv_kept, 3)
                pool.dma_start(kv_new_out, kvsam[:]).then_inc(new_stored, 16)
                pool.dma_start(kwin_p_out, Kwin[:]).then_inc(win_stored, 16)
                pool.dma_start(vwin_p_out, VT[:, NC - 1, :]).then_inc(win_stored, 16)
                for kv in range(KVH):
                    pool.tensor_copy(Ksam[:, kv, :, WINDOW:KS],
                                     KVT[HD * (kv % 2):HD * (kv % 2 + 1), kv // 2, SEQ:T].rearrange("p (b t) -> p b t", b=DEC_BATCH)
                                     ).then_inc(ksam_ready, 1)
                    pool.wait_ge(ksam_ready, kv + 1)

                def scale(j):
                    for h in range(2):
                        pool.wait_ge(den, 2 * (2 * j + h) + 2)
                        by_block = probs[:, h, :].rearrange("p (c k) -> p c k", c=NC)
                        pool.tensor_tensor(by_block, by_block, rden[:, h, :].unsqueeze(2).to_broadcast([P, NC, 2 * L]),
                                           ALU.mult).then_inc(p_ready, 1)
                with pool.Fori(0, NK) as j:
                    scale(j)
                pool.wait_ge(new_stored, 16)
                pool.wait_ge(units_done, PLAN["o"])
                pool.dma_start(Vnew[:], kv_new_out[:, KVH * HD:].rearrange("(b t) v -> t b v", b=DEC_BATCH)).then_inc(vnew_loaded, 16)
                pool.wait_ge(win_stored, 32)

            for k in range(1, NK):
                pool.wait_ge(squared, k)
                pool.wait_ge(sumsq, k)
                pool.tensor_tensor(sqsum[:], sqsum[:], firstsq[:, k - 1, :], ALU.add).then_inc(sumsq, 1)
            squares(1, TILE["down0"])
            pool.dma_start(kv_kept_out, cache_kv[:, :, DEC_SEQ:WINDOW, :]).then_inc(cache_moved, 16)
            prepare_mixer()
            for c in range(2 * GROUPS):
                if c:
                    n = PLAN["bc"] + c + 2
                    pool.wait_ge(weights_lo, n)
                    pool.wait_ge(weights_hi, n + 1)
                    pool.tensor_tensor(wlo[n % 2][:], wraw[n % 2][:], whi[n % 2][:].bitcast(F32),
                                       ALU.subtract).then_inc(weights_lo, 1)
                keep_rows(NX + c, c, TILE["bc"] + c)
            heads()
            squares(2, TILE["out"])
            squares(3, TILE["down1"])
            squares(4, TILE["down2"])
            prepare_attention()
            attention()
            squares(5, TILE["o"])
            squares(6, TILE["down3"])
            for k in range(NK):
                pool.wait_ge(y_ready, k + 1)
                pool.dma_start(y_out[:, k, :], ybuf[:, k, :]).then_inc(y_stored, 16)
            pool.wait_ge(y_stored, 16 * NK)
            pool.wait_ge(cache_moved, 16)


def units(w):
    K, M = w.shape
    kt = K // P
    kp = -(-kt // UNIT) * UNIT
    out = np.zeros((M // P, kp // UNIT, P, UNIT, P), w.dtype)
    v = w.reshape(kt, P, M // P, P).transpose(2, 1, 0, 3)
    for a in range(kp // UNIT):
        n = min(UNIT, kt - a * UNIT)
        out[:, a, :, :n] = v[:, :, a * UNIT:a * UNIT + n]
    return out.reshape(-1, P, UNIT * P)


def gate_up_units(w):
    u = units(w)
    return np.stack([u[:NF], u[NF:]], 1).reshape(-1, P, UNIT * P)


def columns(v):
    return v.reshape(-1, P).T


def per_feature(v):
    return np.ascontiguousarray(v.T.reshape(-1, P, v.shape[0]).transpose(1, 0, 2))


def kernel(**inputs):
    import concourse.bacc as bacc
    from concourse.bass_utils import run_bass_kernel_spmd

    I = {k: np.asarray(v) for k, v in inputs.items()}
    G = QH // KVH

    w_in = I["ssm_w_in"][0]
    wz, wx, wbc = w_in[:, :D_INNER], w_in[:, D_INNER:2 * D_INNER], w_in[:, 2 * D_INNER:D_INNER + P * NXBC]
    wdt = np.zeros((D_MODEL, P), w_in.dtype)
    wdt[:, :HEADS] = w_in[:, D_INNER + P * NXBC:]
    w_out = units(I["ssm_w_out"][0])
    w_out[1:3] = w_out[2:0:-1].copy()
    by_tile = (KVH // 2, 2, G, HD)
    wq = I["attn_w_q"][0].reshape((D_MODEL,) + by_tile).transpose(0, 3, 1, 2, 4).reshape(D_MODEL, D_MODEL)
    wo = I["attn_w_o"][0].reshape(by_tile + (D_MODEL,)).transpose(2, 0, 1, 3, 4).reshape(D_MODEL, D_MODEL)
    weights = np.concatenate([
        gate_up_units(I["ffn1_w_gu"][0]), units(I["ffn1_w_down"][0]),
        units(wdt), units(wbc), np.stack([units(wx), units(wz)], 1).reshape(-1, P, UNIT * P), w_out,
        gate_up_units(I["ffn2_w_gu"][0]), units(I["ffn2_w_down"][0]), units(I["w_kv"]),
        gate_up_units(I["ffn1_w_gu"][1]), units(I["ffn1_w_down"][1]), units(wq), units(wo),
        gate_up_units(I["ffn2_w_gu"][1]), units(I["ffn2_w_down"][1])])

    params = np.zeros((P, NPARAM), np.float32)
    for at, v in ((G_FFN1, I["ffn1_norm"]), (G_MIX, I["mix_norm"]), (G_FFN2, I["ffn2_norm"]), (G_KV, I["kv_norm"]),
                  (G_FINAL, I["final_norm"]), (G_GATE, I["ssm_gate_norm"]), (G_D, np.repeat(I["ssm_d"], HEAD_DIM)),
                  (G_CONVB, I["ssm_conv_b"])):
        c = columns(v)
        params[:, at:at + c.shape[1]] = c
    params[:, G_CONVW:] = I["ssm_conv_w"][0].reshape(CONV, NXBC, P).transpose(2, 1, 0).reshape(P, -1)

    consts = np.zeros((P, NCONST), np.float32)
    a, s = np.arange(P), np.arange(S)
    same = s[:, None] // DEC_SEQ == s // DEC_SEQ
    consts[:, C_ONES:C_ONES + P] = 1
    consts[:, C_IDENT:C_IDENT + P] = np.eye(P)
    consts[:, C_TRI:C_TRI + P] = a[:, None] <= a
    consts[:, C_STRICT:C_STRICT + P] = a[:, None] > a
    consts[:S, C_TRI_S:C_TRI_S + S] = same & (s[:, None] <= s)
    consts[:S, C_TRI_S + S] = 1
    consts[:S, C_STRICT_S:C_STRICT_S + S] = same & (s[:, None] > s)
    consts[:S, C_BLOCK:C_BLOCK + DEC_BATCH] = s[:, None] // DEC_SEQ == np.arange(DEC_BATCH)

    att = np.zeros((P, NATT), np.float32)
    slopes = (2.0 ** (-8.0 * np.arange(1, QH + 1) / QH)).astype(np.float32)
    dist = WINDOW + a[:, None] - np.arange(2 * L)
    att[:, NEGD:NEGD + 2 * L] = np.where((dist >= 0) & (dist < WINDOW), -dist, MASKED)
    rows = np.arange(P)
    dist = WINDOW + (rows % DEC_SEQ)[:, None] - np.arange(KS)
    bias = -slopes[rows // DEC_SEQ][:, None] * dist.astype(np.float32)
    att[:, BIAS_S:BIAS_S + KS] = np.where((dist >= 0) & (dist < WINDOW), bias, MASKED)
    att[:, SLOPE:SLOPE + QH] = slopes
    att[:, SINK:SINK + QH] = I["attn_sinks"][0]
    att[:, SINK_S] = np.repeat(I["attn_sinks"][0], DEC_SEQ)

    state = I["state_ssm"][0].reshape(DEC_BATCH, NX, P, D_STATE)
    cache_k, cache_v = I["cache_k_win"], I["cache_v_win"]
    arrays = {
        "w": weights,
        "x_in": per_feature(np.concatenate([I["x_prompt"][0], I["x_sample"].reshape(S, D_MODEL)])),
        "params": params, "consts": consts, "att_consts": att,
        "dt_params": np.stack([I["ssm_dt_bias"][0], I["ssm_a_log"][0]], 1),
        "conv_state": I["state_conv"][0].reshape(DEC_BATCH, CONV - 1, NXBC, P).transpose(3, 2, 0, 1),
        "ssm_state": state, "ssm_state_t": state.transpose(3, 1, 0, 2),
        "cache_kt": cache_k.transpose(3, 2, 0, 1),
        "cache_v": cache_v.reshape(DEC_BATCH, WINDOW, -1).transpose(1, 0, 2),
        "cache_kv": np.stack([cache_k, cache_v]).reshape(2, DEC_BATCH, WINDOW, -1),
    }
    arrays = {k: np.ascontiguousarray(v) for k, v in arrays.items()}
    outs = {"y": (P, NK, T), "ssm_p": (NX, P, D_STATE), "ssm_s": (DEC_BATCH, NX, P, D_STATE),
            "conv_p": (P, NXBC, CONV - 1), "conv_s": (P, NXBC, DEC_BATCH, CONV - 1), "kwin_p": (WINDOW, KVH * HD),
            "vwin_p": (WINDOW, KVH * HD), "kv_kept": (2, DEC_BATCH, WINDOW - DEC_SEQ, KVH * HD),
            "kv_new": (S, 2 * KVH * HD)}
    nc = bacc.Bacc("TRN2", target_bir_lowering=False, num_devices=1)
    build(nc, *[nc.dram_tensor(n, v.shape, F32, kind="ExternalInput").ap() for n, v in arrays.items()],
          *[nc.dram_tensor(n, v, F32, kind="ExternalOutput").ap() for n, v in outs.items()])
    r = run_bass_kernel_spmd(nc, [arrays], core_ids=[0]).results[0]

    y = r["y"].transpose(2, 1, 0).reshape(T, D_MODEL)
    heads = (1, DEC_BATCH, HEADS, HEAD_DIM, D_STATE)
    new = r["kv_new"].reshape(DEC_BATCH, DEC_SEQ, 2, KVH * HD).transpose(2, 0, 1, 3)
    k_s, v_s = np.concatenate([r["kv_kept"], new], 2).reshape(2, DEC_BATCH, WINDOW, KVH, HD)
    return (y[:SEQ].reshape(1, SEQ, D_MODEL), y[SEQ:].reshape(DEC_BATCH, DEC_SEQ, D_MODEL),
            r["ssm_p"].reshape((1, 1) + heads[2:]), r["conv_p"].transpose(2, 1, 0).reshape(1, 1, CONV - 1, P * NXBC),
            r["kwin_p"].reshape(1, WINDOW, KVH, HD), r["vwin_p"].reshape(1, WINDOW, KVH, HD),
            r["ssm_s"].reshape(heads), r["conv_s"].transpose(2, 3, 1, 0).reshape(1, DEC_BATCH, CONV - 1, P * NXBC),
            k_s, v_s)
```

```python
from contextlib import ExitStack

import numpy as np
import concourse.bass as bass
from concourse import mybir

F32 = mybir.dt.float32
F32R = mybir.dt.float32r
ALU = mybir.AluOpType
ACT = mybir.ActivationFunctionType

P = 128
D_MODEL, D_FF = 1024, 2816
SEQ, DEC_BATCH, DEC_SEQ = 512, 8, 8
S = DEC_BATCH * DEC_SEQ
T = SEQ + S
HALF = T // 2
NK = D_MODEL // P
NF = D_FF // P
D_INNER, HEADS, HEAD_DIM, GROUPS, D_STATE = 2048, 32, 64, 4, 128
CONV = 4
NX = D_INNER // P
NXBC = NX + 2 * GROUPS
L = 128
NC = SEQ // L
KVH, QH, HD, WINDOW = 4, 16, 64, 128
EPS = 1e-5
UNIT = 8
NK_DVE = 6

G_FFN1, G_MIX, G_FFN2, G_KV, G_FINAL = 0, 16, 32, 48, 56
G_GATE, G_D, G_CONVB, G_CONVW = 64, 80, 96, 120
NPARAM = G_CONVW + CONV * NXBC
C_ONES, C_IDENT, C_TRI, C_STRICT, C_TRI_S, C_STRICT_S, C_BLOCK = 0, 128, 256, 384, 512, 577, 641
NCONST = 649
KS = WINDOW + DEC_SEQ
NEGD, BIAS_S, SLOPE, SINK, SINK_S = 0, 2 * L, 2 * L + KS, 2 * L + KS + QH, 2 * L + KS + 2 * QH
NATT = SINK_S + 1
MASKED = -1e30
CBUF = 3 + SEQ + DEC_BATCH * (3 + DEC_SEQ)
CLEN = CBUF - 3
ES = SEQ + S + 4


def down_widths(k_tiles):
    return [min(UNIT, k_tiles - a) for a in range(0, k_tiles, UNIT)]


def unit_plan():
    plan, n = {}, 0
    for name, units in [("gu0", 2 * NF), ("down0", NK * 3), ("dt", 1), ("bc", 2 * GROUPS), ("xz", 2 * NX),
                        ("out", NK * 2), ("gu1", 2 * NF), ("down1", NK * 3), ("kv", 4), ("gu2", 2 * NF),
                        ("down2", NK * 3), ("q", NK), ("o", NK), ("gu3", 2 * NF), ("down3", NK * 3)]:
        plan[name] = n
        n += units
    plan["end"] = n
    return plan


PLAN = unit_plan()


def tile_plan():
    plan, m = {}, 0
    for name, tiles in [("gu0", 2 * NF), ("down0", NK), ("dt", 1), ("bc", 2 * GROUPS + 1), ("xz", 2 * NX), ("out", NK),
                        ("gu1", 2 * NF), ("down1", NK), ("kv", 4), ("gu2", 2 * NF), ("down2", NK), ("q", NK),
                        ("o", NK), ("gu3", 2 * NF), ("down3", NK)]:
        plan[name] = m
        m += tiles
    return plan


TILE = tile_plan()
XG = {"gu0": 0, "dt": 1, "gu1": 2, "kv": 3, "gu2": 4, "q": 5, "gu3": 6}
NORM = {"gu0": 0, "dt": 1, "gu1": 2, "kv": 3, "q": 4, "gu3": 5, "final": 6}


SBUF_BASE, SBUF_END = 16512, 229344


class Map:

    def __init__(self, nc, at):
        self.nc, self.at = nc, at

    def __call__(self, name, shape, dt=F32):
        t = self.nc.alloc_sbuf_tensor_at(name, shape, dt, offset=self.at)
        self.at += -(-4 * int(np.prod(shape[1:])) // 32) * 32
        assert self.at <= SBUF_END, (name, self.at - SBUF_END)
        return t


def build(nc, w, x_in, params, consts, att_consts, dt_params, conv_state, ssm_state, ssm_state_t, cache_kt, cache_v,
          cache_kv, y_out, ssm_p_out, ssm_s_out, conv_p_out, conv_s_out, kwin_p_out, vwin_p_out, kv_kept_out,
          kv_new_out):
    with ExitStack() as ctx:
        sb = Map(nc, SBUF_BASE)
        x = sb("x", [P, NK, T])
        xhi = sb("xhi", [P, NK, T], F32R)
        xlo = sb("xlo", [P, NK, T], F32R)
        wraw = [sb(f"wraw{s}", [P, UNIT * P]) for s in range(2)]
        whi = [sb(f"whi{s}", [P, UNIT * P], F32R) for s in range(2)]
        wlo = [sb(f"wlo{s}", [P, UNIT * P], F32R) for s in range(2)]
        rstd = sb("rstd", [P, T])
        prm = sb("prm", [P, NPARAM])
        strict_r = nc.alloc_sbuf_tensor_at("strict_r", [P, P], F32R, offset=sb.at + 4 * C_STRICT)
        cst = sb("cst", [P, NCONST])
        sqsum = sb("sqsum", [P, T])
        th = sb("th", [P, CBUF])
        sq = th[:, 0:T]
        ones_r = sb("ones_r", [P, 3 * HEAD_DIM], F32R)
        arena = sb.at
        ffn = Map(nc, arena)
        hhi = ffn("hhi", [P, NF, T], F32R)
        hlo = ffn("hlo", [P, NF, T], F32R)
        gate = ffn("gate", [P, T])
        silu = ffn("silu", [P, T])
        up = ffn("up", [P, T])
        hidden = ffn("hidden", [P, T])
        firstsq = nc.alloc_sbuf_tensor_at("firstsq", [P, NK - 1, T], F32, offset=arena + 4 * T * (NF - NK + 1))
        mam = Map(nc, arena)
        yall = mam("yall", [P, NX, T])
        CT = mam("CT", [P, GROUPS, T])
        Btm = mam("Btm", [P, GROUPS, NC + 1, P])
        cbm = mam("cbm", [P, GROUPS, T])
        Bm = mam("Bm", [S, DEC_BATCH, P])
        E = mam("E", [P, 2, ES])
        E2 = mam("E2", [P, T])
        xdt = mam("xdt", [P, NC + 1, P])
        xdd = mam("xdd", [P, NC + 1, P])
        yo = nc.alloc_sbuf_tensor_at("yo", [P, T], F32, offset=mam.at - 4 * P * (NC + 1))
        hT = nc.alloc_sbuf_tensor_at("hT", [P, NC - 1, P], F32, offset=mam.at - 4 * P * (NC + 1))
        hst = mam("hst", [P, NC, P])
        h0s = mam("h0s", [P, DEC_BATCH, P])
        h0T = mam("h0T", [P, DEC_BATCH, P])
        cbuf = mam("cbuf", [P, CBUF])
        cacc = mam("cacc", [P, CBUF])
        xs = mam("xs", [P, T])
        yd = sqsum
        gsum = mam("gsum", [P, GROUPS, T])
        dahi = nc.alloc_sbuf_tensor_at("dahi", [P, NC + 1, 2 * HEADS], F32R, offset=mam.at)[:, 0:NC, HEADS:]
        dT = mam("dT", [P, NC + 1, 2 * HEADS])
        cacc2 = nc.alloc_sbuf_tensor_at("cacc2", [P, CBUF], F32, offset=mam.at)
        seghi = mam("seghi", [P, 2, NC, P], F32R)
        seglo = mam("seglo", [P, 2, NC, P], F32R)
        segs = mam("segs", [S, 2, S + 1])
        dalo = mam("dalo", [P, NC, HEADS], F32R)
        cstate = mam("cstate", [P, NXBC, DEC_BATCH, 3])
        cnew = mam("cnew", [P, NXBC, 3])
        pre = Map(nc, arena)
        BT = pre("BT", [P, GROUPS, T])
        dtp = pre("dtp", [2 * HEADS, T])
        dts = [pre(f"dts{i}", [HEADS, T]) for i in range(5)]
        dtprm = pre("dtprm", [HEADS, 4])
        post = Map(nc, arena)
        ylo = post("ylo", [P, NX, T], F32R)
        yhi = post("yhi", [P, NX, T], F32R)
        ybuf = nc.alloc_sbuf_tensor_at("ybuf", [P, NK, T], F32, offset=arena)

        KVT = ffn("KVT", [P, 4, T])
        att = Map(nc, arena)
        ohi = att("ohi", [P, NK, T], F32R)
        olo = att("olo", [P, NK, T], F32R)
        qs = att("qs", [P, T])
        VT = att("VT", [P, NC, KVH * HD])
        Kwin = att("Kwin", [P, KVH * HD])
        kvsam = att("kvsam", [S, 2 * KVH * HD])
        sc_at = att.at
        sc = att("sc", [P, 2, 2 * SEQ])
        probs = att("probs", [P, 2, 2 * SEQ])
        nmax, rsum, esink, rden = (att(v, [P, 2, NC]) for v in ("nmax", "rsum", "esink", "rden"))
        Qsam = att("Qsam", [HD, KVH, DEC_BATCH, QH // KVH, DEC_SEQ])
        snmax, srsum, sesink, srden = (att(v, [P, DEC_BATCH]) for v in ("snmax", "srsum", "sesink", "srden"))
        attc = att("attc", [P, NATT])
        pt_at = att.at
        PT = att("PT", [P, 2, 2 * NC - 1, P])
        Vsam = att("Vsam", [P, DEC_BATCH, KVH * HD])
        Ksam = att("Ksam", [HD, KVH, DEC_BATCH, KS])
        PTn = att("PTn", [DEC_SEQ, DEC_BATCH, P])
        assert att.at <= arena + 4 * T * (2 * NF + 4)
        psam = nc.alloc_sbuf_tensor_at("psam", [P, DEC_BATCH, KS], F32, offset=sc_at)
        PTs = nc.alloc_sbuf_tensor_at("PTs", [P, DEC_BATCH, P], F32, offset=pt_at)
        Vnew = nc.alloc_sbuf_tensor_at("Vnew", [DEC_SEQ, DEC_BATCH, KVH * HD], F32, offset=SBUF_BASE + 4 * NK * T)
        ssam = nc.alloc_sbuf_tensor_at("ssam", [P, DEC_BATCH, KS], F32, offset=SBUF_BASE + 4 * NK * T + 4 * DEC_BATCH * KVH * HD)
        negd = attc[:, NEGD:NEGD + 2 * L]

        psum = ctx.enter_context(nc.psum_tensor("psum", [P, 8, 512], F32))
        acc = psum[:, 0:4, :]
        nrm = psum[:, 4:6, :]
        bank = [psum[:, b, :] for b in range(8)]

        def sem(name):
            return ctx.enter_context(nc.semaphore(name))

        raw_loaded = [sem("raw_loaded0"), sem("raw_loaded1")]
        weights_hi = sem("weights_hi")
        weights_lo = sem("weights_lo")
        units_done = sem("units_done")
        evicted = sem("evicted")
        x_loaded = [sem(f"x_loaded{k}") for k in range(NK)]
        prm_loaded, c_loaded = sem("prm_loaded"), sem("c_loaded")
        xg_hi = sem("xg_hi")
        xg_used = sem("xg_used")
        xg_lo = sem("xg_lo")
        squared = sem("squared")
        sumsq = sem("sumsq")
        norm_sum = sem("norm_sum")
        var_ready = sem("var_ready")
        std_ready = sem("std_ready")
        rstd_ready = sem("rstd_ready")
        silu_ready = sem("silu_ready")
        h_ready = sem("h_ready")
        h_hi = sem("h_hi")
        h_lo = sem("h_lo")
        last_square = sem("last_square")
        y_gained = sem("y_gained")
        y_ready = sem("y_ready")
        y_ready_pool = sem("y_ready_pool")
        conv_prm = sem("conv_prm")
        st_loaded = sem("st_loaded")
        conv_step = sem("conv_step")
        conv_tanh = sem("conv_tanh")
        conv_done = sem("conv_done")
        conv_saved = sem("conv_saved")
        cleared = sem("cleared")
        dt_act = sem("dt_act")
        dt_dve = sem("dt_dve")
        dt_turned = sem("dt_turned")
        ones_set = sem("ones_set")
        consts_r = sem("consts_r")
        dt_kept = sem("dt_kept")
        b_turned, cb_done = sem("b_turned"), sem("cb_done")
        b_kept = sem("b_kept")
        cb_kept = sem("cb_kept")
        bm_ready = sem("bm_ready")
        z_tanh, z_ready = sem("z_tanh"), sem("z_ready")
        seg_lhs = sem("seg_lhs")
        x_turned = sem("x_turned")
        seg_ready = sem("seg_ready")
        decay_ready = sem("decay_ready")
        xdt_ready, xdd_ready = sem("xdt_ready"), sem("xdd_ready")
        m_ready = sem("m_ready")
        s_ready, ss_ready = sem("s_ready"), sem("ss_ready")
        h_step = sem("h_step")
        h0_loaded, h0t_loaded = sem("h0_loaded"), sem("h0t_loaded")
        h0_decayed = sem("h0_decayed")
        ss_final = sem("ss_final")
        h_turned = sem("h_turned")
        hT_ready = sem("hT_ready")
        ssd_done = sem("ssd_done")
        skip_ready = sem("skip_ready")
        y_step = sem("y_step")
        ysq, gsum_step = sem("ysq"), sem("gsum_step")
        hp_stored, hs_stored = sem("hp_stored"), sem("hs_stored")
        cnew_stored = sem("cnew_stored")
        gnorm_sum = sem("gnorm_sum")
        gvar, gstd, grstd = sem("gvar"), sem("gstd"), sem("grstd")
        yn_ready, y_hi, y_lo = sem("yn_ready"), sem("y_hi"), sem("y_lo")
        y_stored = sem("y_stored")

        def out_of(pair):
            return acc[:, 2 * pair:2 * pair + 2, 0:HALF]

        def halves(ap):
            return ap.rearrange("p (a n) -> p a n", a=2)

        kv_turned = sem("kv_turned")
        kv_kept = sem("kv_kept")
        scores_done = sem("scores_done")
        soft = sem("soft")
        p_exp = sem("p_exp")
        den = sem("den")
        p_ready = sem("p_ready")
        p_turned, pt_ready = sem("p_turned"), sem("pt_ready")
        pv_done = sem("pv_done")
        o_hi, o_lo = sem("o_hi"), sem("o_lo")
        qsam_ready = sem("qsam_ready")
        ksam_ready = sem("ksam_ready")
        ssc_done = sem("ssc_done")
        ssoft = sem("ssoft")
        sp_exp, sden, sp_ready = sem("sp_exp"), sem("sden"), sem("sp_ready")
        sp_turned, spt_ready, spv_done = sem("sp_turned"), sem("spt_ready"), sem("spv_done")
        kcache_loaded, vsam_loaded, vnew_loaded = sem("kcache_loaded"), sem("vsam_loaded"), sem("vnew_loaded")
        att_loaded, att_cleared = sem("att_loaded"), sem("att_cleared")
        win_stored, new_stored, cache_moved = sem("win_stored"), sem("new_stored"), sem("cache_moved")

        block = ctx.enter_context(nc.Block())

        def column(at, c, stride=1):
            return prm[:, at + c * stride:at + c * stride + 1] if isinstance(c, int) else prm[:, bass.ds(c * stride + at, 1)]

        def acol(at, head):
            return attc[:, at + head:at + head + 1] if isinstance(head, int) else attc[:, bass.ds(head + at, 1)]

        def sample_out(kp, h):
            own = bank[3 + kp][HD * h:HD * (h + 1), :].rearrange("p (b k r) -> p k b r", b=DEC_BATCH, k=2)[:, h]
            return own.rearrange("p b (g t) -> p g b t", g=QH // KVH)

        @block.sync
        def _(sp):
            sp.dma_start(wraw[0][:], w[0]).then_inc(raw_loaded[0], 16)
            for k in range(NK):
                sp.dma_start(x[:, k, :], x_in[:, k, :]).then_inc(x_loaded[k], 16)
                if k == 1:
                    sp.dma_start(wraw[1][:], w[1]).then_inc(raw_loaded[1], 16)
            pairs = (PLAN["end"] - 2) // 2
            with sp.Fori(0, pairs) as i:
                for s in range(2):
                    sp.wait_ge(weights_lo, 2 * i + s + 1)
                    sp.dma_start(wraw[s][:], w[2 * i + 2 + s]).then_inc(raw_loaded[s], 16)
            for n in range(2 * pairs + 2, PLAN["end"]):
                sp.wait_ge(weights_lo, n - 1)
                sp.dma_start(wraw[n % 2][:], w[n]).then_inc(raw_loaded[n % 2], 16)
            for i in range(max(NK_DVE, NK - NK_DVE)):
                if i < NK_DVE:
                    sp.wait_ge(y_ready, i + 1)
                    sp.dma_start(y_out[:, i, :], ybuf[:, i, :]).then_inc(y_stored, 16)
                if i % 2 == 1 and NK_DVE + i // 2 < NK:
                    sp.wait_ge(y_ready_pool, i // 2 + 1)
                    sp.dma_start(y_out[:, NK_DVE + i // 2, :], ybuf[:, NK_DVE + i // 2, :]).then_inc(y_stored, 16)
            sp.wait_ge(y_stored, 16 * NK)

        ident = cst[:, C_IDENT:C_IDENT + P]
        tri = cst[:, C_TRI:C_TRI + P]
        strict = cst[:, C_STRICT:C_STRICT + P]
        tri_s = cst[0:S, C_TRI_S:C_TRI_S + S + 1]
        strict_s = cst[0:S, C_STRICT_S:C_STRICT_S + S]
        in_seq = cst[0:S, C_BLOCK:C_BLOCK + DEC_BATCH]

        @block.tensor
        def _(pe):
            def unit(n, step, width, pair, hi, lo, k0, start, stop, k_wait=None, norm_after=None, used=None):
                s = n % 2
                pe.wait_ge(weights_lo, n + step + 1)
                last = None
                for k in range(width):
                    if k_wait is not None:
                        pe.wait_ge(k_wait[0], k_wait[1] + k + 1)
                    products = ((whi, hi), (whi, lo), (wlo, hi))
                    for i, (wt, m) in enumerate(products):
                        for half in range(2):
                            last = pe.matmul(acc[:, 2 * pair + half, 0:HALF], wt[s][:, k * P:(k + 1) * P],
                                             m[:, k0 + k, half * HALF:(half + 1) * HALF],
                                             start=start and k == 0 and i == 0,
                                             stop=stop and k == width - 1 and i == 2)
                    if used is not None and k < width - 1:
                        last.then_inc(used, 1)
                    if norm_after is not None and k == 5:
                        norm(norm_after)
                last.then_inc(units_done, 1)

            def half_unit(n, step, pair, part, rhs=(xhi, xlo)):
                s = n % 2
                if part == 0:
                    pe.wait_ge(weights_lo, n + step + 1)
                for k in range(4 * part, 4 * part + 4):
                    for i, (wt, m) in enumerate(((whi, rhs[0]), (whi, rhs[1]), (wlo, rhs[0]))):
                        for half in range(2):
                            last = pe.matmul(acc[:, 2 * pair + half, 0:HALF], wt[s][:, k * P:(k + 1) * P],
                                             m[:, k, half * HALF:(half + 1) * HALF],
                                             start=k == 0 and i == 0, stop=k == NK - 1 and i == 2)
                if part == 1:
                    last.then_inc(units_done, 1)

            def norm(e):
                pe.wait_ge(sumsq, NK * (e + 1))
                if e == 0:
                    pe.wait_ge(c_loaded, 16)
                for half in range(2):
                    last = pe.matmul(nrm[:, half, 0:HALF], cst[:, C_ONES:C_ONES + P], sqsum[:, half * HALF:(half + 1) * HALF],
                                     start=True, stop=True)
                last.then_inc(norm_sum, 1)

            def last_norm():
                for src, first in ((sqsum, True), (sq, False)):
                    if first:
                        pe.wait_ge(sumsq, NK * NORM["final"] + NK - 1)
                    else:
                        pe.wait_ge(last_square, 1)
                    for half in range(2):
                        last = pe.matmul(nrm[:, half, 0:HALF], cst[:, C_ONES:C_ONES + P],
                                         src[:, half * HALF:(half + 1) * HALF], start=first, stop=not first)
                last.then_inc(norm_sum, 1)

            def gate_up(ph, with_norm=True):
                n, m = PLAN[ph], TILE[ph]

                def body(i, first=False):
                    for u in range(2):
                        pe.wait_ge(evicted, m + 2 * i + u + 1)
                        unit(n + u, 2 * i, NK, (m + u) % 2, xhi, xlo, 0, True, True,
                             (xg_lo, NK * XG[ph]) if first and u == 0 else None,
                             norm_after=NORM[ph] if first and u == 0 and with_norm else None)
                body(0, True)
                with pe.Fori(1, NF) as i:
                    body(i)

            def residual(ph, widths, hi, lo, ready, before, kwise=False, done=0):
                n, m, per = PLAN[ph], TILE[ph], len(widths)

                def body(i):
                    for d in range(2):
                        pe.wait_ge(evicted, m + 2 * i + d + 1)
                        for a, width in enumerate(widths):
                            if not kwise:
                                pe.wait_ge(ready, before + UNIT * a + width)
                            unit(n + per * d + a, 2 * per * i, width, (m + d) % 2, hi, lo, UNIT * a, a == 0,
                                 a == per - 1)
                if kwise:
                    for a, width in enumerate(widths):
                        for d in range(2):
                            unit(n + 2 * a + d, 0, width, d, hi, lo, UNIT * a, a == 0, a == per - 1,
                                 (ready, before + UNIT * a) if d == 0 else None)
                            if a == d == 0:
                                group_sum(GROUPS - 1, 6)
                with pe.Fori(1 if kwise else done, NK // 2) as i:
                    body(i)

            def key_value():
                n, m = PLAN["kv"], TILE["kv"]
                for c in range(4):
                    pe.wait_ge(evicted, m + c + 1)
                    unit(n + c, 0, NK, (m + c) % 2, xhi, xlo, 0, True, True,
                         (xg_lo, NK * XG["kv"]) if c == 0 else None, norm_after=NORM["kv"] if c == 0 else None,
                         used=xg_used if c == 3 else None)

            def b_and_c():
                pe.wait_ge(evicted, TILE["dt"] + 1)
                unit(PLAN["dt"], 0, NK, 0, xhi, xlo, 0, True, True, (xg_lo, NK * XG["dt"]), norm_after=NORM["dt"])
                for c in range(2 * GROUPS):
                    pe.wait_ge(evicted, TILE["bc"] + c + 1)
                    unit(PLAN["bc"] + c, 0, NK, (c + 1) % 2, xhi, xlo, 0, True, True)

            def b_c_products():
                pe.wait_ge(rstd_ready, NORM["dt"] + 1)
                for g in range(GROUPS):
                    b = 2 + 3 * (g % 2)
                    pe.wait_ge(conv_done, 2 * (GROUPS + g) + 2)
                    if g == 0:
                        pe.wait_ge(evicted, TILE["xz"] + 3)
                    if g == 1:
                        pe.wait_ge(dt_kept, 4)
                    if g >= 2:
                        pe.wait_ge(b_kept, 2 * g - 2)
                        pe.wait_ge(cb_kept, 2 * g - 2)
                    for c in range(NC):
                        pe.transpose(bank[b][:, c * L:(c + 1) * L], BT[:, g, c * L:(c + 1) * L], ident)
                    pe.transpose(bank[b + 1][0:S, 0:P], BT[:, g, SEQ:T], ident).then_inc(b_turned, 1)
                    for c in range(NC):
                        cols = slice(c * L, (c + 1) * L)
                        pe.matmul(bank[b + 2][:, cols], BT[:, g, cols], CT[:, g, cols], start=True, stop=True)
                    pe.wait_ge(b_kept, 2 * g + 2)
                    pe.matmul(bank[b + 1][0:S, P:P + S], BT[:, g, SEQ:T], CT[:, g, SEQ:T], start=True,
                              stop=True).then_inc(cb_done, 1)

            def turn_dt():
                pe.wait_ge(dt_dve, 7)
                for c in range(NC):
                    pe.transpose(bank[7][:, c * 64:(c + 1) * 64], dtp[:, c * L:(c + 1) * L], ident[0:64, 0:64])
                pe.transpose(bank[7][0:S, 256:320], dtp[:, SEQ:T], ident[0:64, 0:64]).then_inc(dt_turned, 1)

            def decays(p, first):
                pe.wait_ge(conv_done, 2 * (2 * GROUPS + p) + 2)
                if not first:
                    pe.wait_ge(hT_ready, p)
                if not first:
                    pe.wait_ge(y_step, 5 * p - 2)
                for c in range(NC):
                    pe.transpose(bank[5][:, c * L:(c + 1) * L], xs[:, c * L:(c + 1) * L], ident)
                pe.transpose(bank[7][0:S, 0:P], xs[:, SEQ:T], ident).then_inc(x_turned, 1)
                pe.wait_ge(seg_lhs, 3 * p + 3)
                if not first:
                    pe.wait_ge(h_step, 4 * p)
                if not first:
                    pe.wait_ge(ss_final, p)
                for h in range(2):
                    for part, seg in enumerate((seghi, seglo)):
                        pe.matmul(bank[2 + h][:, :], strict_r[:], seg[:, h, :, :].rearrange("p c t -> p (c t)"),
                                  start=part == 0, stop=part == 1)
                pe.matmul(bank[6][0:S, 0:2 * (S + 1)], strict_s, segs[:].rearrange("p h t -> p (h t)"),
                          start=True, stop=True)
                for h in range(2):
                    for part, seg in enumerate((seghi, seglo)):
                        pe.matmul(bank[4][:, :], ones_r[:, (1 - h) * HEAD_DIM:(1 - h) * HEAD_DIM + P], seg[:, h, :, :].rearrange("p c t -> p (c t)"),
                                  start=h == part == 0, stop=h == part == 1)
                for h in range(2):
                    last = pe.matmul(bank[6][h * HEAD_DIM:(h + 1) * HEAD_DIM, 144:144 + S],
                                     cst[0:S, C_ONES:C_ONES + HEAD_DIM], segs[:, h, 0:S], start=True, stop=True)
                last.then_inc(seg_ready, 1)

            def states(p, g):
                pe.wait_ge(decay_ready, 5 * p + 5)
                pe.wait_ge(xdd_ready, 2 * p + 2)
                for c in range(NC):
                    last = pe.matmul(bank[2][:, c * P:(c + 1) * P], xdd[:, c, :], Btm[:, g, c, :], start=True, stop=True)
                last.then_inc(s_ready, 1)
                pe.wait_ge(bm_ready, g + 1)
                for b in range(2):
                    last = pe.matmul(bank[3 + b][:, :], xdd[0:S, NC, :], Bm[:, 4 * b:4 * b + 4, :], start=True, stop=True)
                last.then_inc(ss_ready, 1)

            def turn_states(p):
                pe.wait_ge(h_step, 4 * p + 3)
                pe.wait_ge(xdt_ready, 2 * p + 2)
                for c in range(NC - 1):
                    last = pe.transpose(bank[5][:, c * P:(c + 1) * P], hst[:, c, :], ident)
                last.then_inc(h_turned, 1)

            def outputs(p, g):
                pe.wait_ge(hT_ready, p + 1)
                pe.wait_ge(m_ready, p + 1)
                pe.wait_ge(h0t_loaded, 16 * p + 16)
                for c in range(1, NC):
                    pe.matmul(bank[6][:, (c - 1) * L:c * L], hT[:, c - 1, :], CT[:, g, c * L:(c + 1) * L],
                              start=True, stop=True)
                for b in range(DEC_BATCH):
                    at = SEQ + b * DEC_SEQ
                    pe.matmul(bank[6][:, at - L:at - L + DEC_SEQ], h0T[:, b, :], CT[:, g, at:at + DEC_SEQ],
                              start=True, stop=True)
                for h in range(2):
                    rows = slice(h * HEAD_DIM, (h + 1) * HEAD_DIM)
                    pe.matmul(bank[6][rows, 448:512], xdt[0:S, NC, rows], E[0:S, h, SEQ:T], start=True, stop=True)
                    for c in range(NC):
                        cols = slice(c * L, (c + 1) * L)
                        last = pe.matmul(bank[7][rows, cols], xdt[:, c, rows], E[:, h, cols], start=True, stop=True)
                last.then_inc(ssd_done, 1)

            def heads():
                n, m = PLAN["xz"], TILE["xz"]

                def body(p, g, first=False, more=True, stats=None):
                    if more:
                        pe.wait_ge(evicted, m + 2 * p + 3)
                        half_unit(n + 1, 2 * p, 0, 0)
                    if first:
                        half_unit(n + 1, 0, 0, 1)
                    decays(p, first)
                    if more and not first:
                        half_unit(n + 1, 2 * p, 0, 1)
                    if not more:
                        pe.wait_ge(evicted, m + 2 * p + 3)
                        half_unit(n + 1, 2 * p, 0, 0)
                    states(p, g)
                    if more:
                        pe.wait_ge(evicted, m + 2 * p + 4)
                        if stats is not None:
                            group_sum(stats, 0)
                            pe.wait_ge(gvar, stats + 1)
                        half_unit(n + 2, 2 * p, 0, 0)
                        turn_states(p)
                        half_unit(n + 2, 2 * p, 0, 1)
                    else:
                        half_unit(n + 1, 2 * p, 0, 1)
                        turn_states(p)
                    outputs(p, g)

                pe.wait_ge(evicted, m)
                half_unit(n, 0, 1, 0)
                half_unit(n, 0, 1, 1)
                turn_dt()
                b_c_products()
                pe.wait_ge(consts_r, 2)
                body(0, 0, first=True)
                with pe.Fori(1, 4) as p:
                    body(p, 0)
                with pe.Fori(1, GROUPS - 1) as g:
                    with pe.Fori(0, 4) as q:
                        body(g * 4 + q, g)
                with pe.Fori(0, GROUPS - 1) as q:
                    body(q + 12, GROUPS - 1, stats=q)
                body(NX - 1, GROUPS - 1, more=False)

            def group_sum(g, b):
                if b == 6:
                    pe.wait_ge(y_step, 5 * NX)
                pe.wait_ge(gsum_step, 4 * g + 4)
                for half in range(2):
                    last = pe.matmul(psum[:, b + half, 0:HALF], cst[:, C_ONES:C_ONES + P],
                                     gsum[:, g, half * HALF:(half + 1) * HALF], start=True, stop=True)
                last.then_inc(gnorm_sum, 1)

            def mixer_out():
                pe.wait_ge(evicted, TILE["out"] + 2)
                residual("out", [NK, NK], yhi, ylo, y_lo, 0, kwise=True)

            def turn_keys_values():
                for c in range(2):
                    for b in range(NC):
                        pe.transpose(psum[:, 2 + b // 2, (b % 2) * 256 + c * P:(b % 2) * 256 + (c + 1) * P],
                                     KVT[:, 2 + c, b * L:(b + 1) * L], ident)
                    pe.transpose(bank[6][:, c * P:(c + 1) * P], KVT[:, c, SEQ - L:SEQ], ident)
                for c in range(4):
                    last = pe.transpose(bank[7][0:S, c * P:(c + 1) * P], KVT[:, c, SEQ:T], ident)
                last.then_inc(kv_turned, 1)

            def scores(j, kp):
                pe.wait_ge(evicted, TILE["q"] + j + 3)
                for h in range(2):
                    rows = slice(HD * h, HD * (h + 1))
                    if h == 1:
                        pe.wait_ge(pt_ready, 2 * j)
                    for c in range(NC):
                        at = 2 * L * c
                        keys = slice(max(c - 1, 0) * L, (c + 1) * L)
                        lo_col = at if c else L
                        last = pe.matmul(psum[:, 2 + 2 * h + lo_col // 512, lo_col % 512:lo_col % 512 + (keys.stop - keys.start)],
                                         qs[rows, c * L:(c + 1) * L], KVT[rows, kp, keys], start=True, stop=True)
                    last.then_inc(scores_done, 1)

            def turn_probs(j):
                for h in range(2):
                    pe.wait_ge(p_ready, 2 * j + h + 1)
                    if h == 0:
                        pe.wait_ge(o_lo, j)
                    for t in range(2 * NC - 1):
                        last = pe.transpose(psum[:, (6 if h == 0 else 4) + t // 4, (t % 4) * P:(t % 4 + 1) * P],
                                            probs[:, h, (t + 1) * P:(t + 2) * P], ident)
                    last.then_inc(p_turned, 1)

            def weigh_values(j, kp):
                pe.wait_ge(pt_ready, 2 * j + 2)
                for h in range(2):
                    v = slice((2 * kp + h) * HD, (2 * kp + h + 1) * HD)
                    for c in range(NC):
                        out = bank[6][HD * h:HD * (h + 1), c * L:(c + 1) * L]
                        if c:
                            pe.matmul(out, VT[:, c - 1, v], PT[:, h, 2 * c - 1, :], start=True, stop=False)
                        last = pe.matmul(out, VT[:, c, v], PT[:, h, 2 * c, :], start=c == 0, stop=True)
                last.then_inc(pv_done, 1)

            def attention():
                n, m = PLAN["q"], TILE["q"]

                def body(g, kp, first=False):
                    j = 2 * g + kp
                    pe.wait_ge(evicted, m + j + (1 if first else 2))
                    unit(n + kp, 2 * g, NK, 0, xhi, xlo, 0, True, True, (xg_lo, NK * XG["q"]) if first else None,
                         norm_after=NORM["q"] if first else None)
                    if first:
                        turn_keys_values()
                        pe.wait_ge(kv_kept, 3)
                    else:
                        turn_probs(j - 1)
                    scores(j, kp)
                    if not first:
                        weigh_values(j - 1, 1 - kp)

                body(0, 0, first=True)
                body(0, 1)
                with pe.Fori(1, QH // KVH) as g:
                    body(g, 0)
                    body(g, 1)
                sample_scores()
                turn_probs(NK - 1)
                weigh_values(NK - 1, 1)

            def sample_scores():
                pe.wait_ge(soft, 4 * (2 * NK - 2) + 2)
                pe.wait_ge(qsam_ready, NK * 2)
                pe.wait_ge(ksam_ready, KVH)
                pe.wait_ge(kcache_loaded, 16)
                for b in range(DEC_BATCH):
                    for kv in range(KVH):
                        last = pe.matmul(psum[32 * kv:32 * kv + 32, b // 3, (b % 3) * KS:(b % 3 + 1) * KS],
                                         Qsam[:, kv, b, :, :].rearrange("p g t -> p (g t)"), Ksam[:, kv, b, :],
                                         start=True, stop=True)
                last.then_inc(ssc_done, 1)

            def sample_attention():
                pe.wait_ge(sp_ready, 1)
                pe.wait_ge(o_lo, NK)
                for b in range(DEC_BATCH):
                    pe.transpose(psum[:, 5 + b // 4, (b % 4) * P:(b % 4 + 1) * P], psam[:, b, 0:WINDOW], ident)
                for b in range(DEC_BATCH):
                    last = pe.transpose(psum[0:DEC_SEQ, (7, 2)[b // 4], (b % 4) * P:(b % 4 + 1) * P],
                                        psam[:, b, WINDOW:KS], ident)
                last.then_inc(sp_turned, 1)
                n = PLAN["o"]

                def half_tile(d, half):
                    pe.wait_ge(weights_lo, n + d + 1)
                    s = (n + d) % 2
                    for k in range(NK):
                        for i, (wt, src) in enumerate(((whi, ohi), (whi, olo), (wlo, ohi))):
                            last = pe.matmul(acc[:, 2 * d + half, 0:HALF], wt[s][:, k * P:(k + 1) * P],
                                             src[:, k, half * HALF:(half + 1) * HALF],
                                             start=k == 0 and i == 0, stop=k == NK - 1 and i == 2)
                    if half == 1:
                        last.then_inc(units_done, 1)

                pe.wait_ge(evicted, TILE["o"] + 2)
                half_tile(0, 0)
                pe.wait_ge(spt_ready, 3)
                pe.wait_ge(vsam_loaded, 16)
                pe.wait_ge(vnew_loaded, 16)
                for b in range(DEC_BATCH):
                    for kp in range(2):
                        out = bank[3 + kp][:, b * 64:(b + 1) * 64]
                        v, rows = slice(kp * P, (kp + 1) * P), slice(64 * kp, 64 * kp + 64)
                        pe.matmul(out, Vsam[:, b, v], PTs[:, b, rows], start=True, stop=False)
                        last = pe.matmul(out, Vnew[:, b, v], PTn[:, b, rows], start=False, stop=True)
                last.then_inc(spv_done, 1)
                half_tile(1, 0)
                pe.wait_ge(o_lo, NK + 4)
                half_tile(0, 1)
                half_tile(1, 1)

            gate_up("gu0")
            residual("down0", down_widths(NF), hhi, hlo, h_lo, 0)
            b_and_c()
            heads()
            mixer_out()
            gate_up("gu1")
            residual("down1", down_widths(NF), hhi, hlo, h_lo, NF)
            key_value()
            gate_up("gu2", with_norm=False)
            residual("down2", down_widths(NF), hhi, hlo, h_lo, 2 * NF)
            attention()
            sample_attention()
            residual("o", [NK], ohi, olo, o_lo, 4, done=1)
            gate_up("gu3")
            residual("down3", down_widths(NF), hhi, hlo, h_lo, 3 * NF)
            last_norm()

        @block.scalar
        def _(act):
            act.dma_start(prm[:], params).then_inc(prm_loaded, 16)
            act.dma_start(cst[:], consts).then_inc(c_loaded, 16)

            def split_hi(n, step):
                act.wait_ge(raw_loaded[n % 2], 16 * (n // 2 + 1) + 8 * step)
                if n >= 2:
                    act.wait_ge(units_done, n + step - 1)
                act.activation(whi[n % 2][:], wraw[n % 2][:], ACT.Copy).then_inc(weights_hi, 1)

            def gained(k, gain):
                act.activation(xhi[:, k, :], x[:, k, :], ACT.Copy, scale=prm[:, gain + k:gain + k + 1] if isinstance(k, int)
                               else prm[:, bass.ds(k + gain, 1)]).then_inc(xg_hi, 1)

            def std(e):
                act.wait_ge(var_ready, e + 1)
                act.activation(rstd[:], rstd[:], ACT.Sqrt).then_inc(std_ready, 1)

            def gate_up(ph, before, with_norm=True):
                n, m = PLAN[ph], TILE[ph]

                def body(i, first=False):
                    if first and with_norm:
                        std(NORM[ph])
                    split_hi(n + 2, 2 * i)
                    act.wait_ge(evicted, m + 2 * i + 3)
                    act.wait_ge(h_ready, NF * before + i)
                    act.activation(silu[:], gate[:], ACT.Silu).then_inc(silu_ready, 1)
                    split_hi(n + 3, 2 * i)
                    act.wait_ge(h_ready, NF * before + i + 1)
                    act.activation(hhi[:, i, :], hidden[:], ACT.Copy).then_inc(h_hi, 1)
                body(0, True)
                with act.Fori(1, NF) as i:
                    body(i)

            def residual(ph, per, gain, last=False, kwise=False):
                n, m = PLAN[ph], TILE[ph]

                def body(i, splits=2 * per, skip=0):
                    for d in range(2):
                        for a in range(per):
                            if skip <= per * d + a < splits:
                                split_hi(n + 2 + per * d + a, 2 * per * i)
                        if gain is not None:
                            act.wait_ge(evicted, m + 2 * i + d + 3)
                            gained(2 * i + d, gain)
                if kwise:
                    body(0, skip=2)
                with act.Fori(1 if kwise else 0, NK // 2 - 1) as i:
                    body(i)
                body(NK // 2 - 1, 2 * per - 2 if last else 2 * per)

            def conv_act(c, cacc=cacc):
                act.wait_ge(conv_step, 4 * c + 4)
                act.activation(th[:, 0:CLEN], cacc[:, 0:CLEN], ACT.Tanh).then_inc(conv_tanh, 1)

            def b_and_c():
                n = PLAN["bc"]
                std(NORM["dt"])
                split_hi(PLAN["dt"] + 2, 0)
                for c in range(2 * GROUPS):
                    acc_c = (cacc, cacc2)[c % 2]
                    act.wait_ge(evicted, TILE["bc"] + c + 3)
                    if c >= 2:
                        act.wait_ge(conv_done, 2 * c - 2)
                    act.activation(acc_c[:, 0:CLEN], cbuf[:, 0:CLEN], ACT.Identity, scale=column(G_CONVW, NX + c, CONV),
                                   bias=column(G_CONVB, NX + c)).then_inc(conv_step, 1)
                    split_hi(n + c + 2, 0)
                    if c:
                        act.wait_ge(conv_done, 2 * c)
                    conv_act(c, acc_c)
                    if c in (0, 3):
                        softplus(c // 3)

            def softplus(part):
                s1, e, u, ln, r = dts
                if part == 0:
                    act.wait_ge(st_loaded, 32)
                    act.wait_ge(evicted, TILE["dt"] + 3)
                    act.activation(e[:], s1[:], ACT.Abs, bias=dtprm[:, 0:1]).then_inc(dt_act, 1)
                    act.activation(dtprm[:, 2:3], dtprm[:, 1:2], ACT.Exp).then_inc(dt_act, 1)
                    act.wait_ge(dt_act, 1)
                    act.activation(e[:], e[:], ACT.Exp, scale=-1.0).then_inc(dt_act, 1)
                else:
                    act.wait_ge(dt_dve, 2)
                    act.activation(ln[:], u[:], ACT.Ln).then_inc(dt_act, 1)
                    act.wait_ge(dt_act, 4)
                    act.activation(r[:], ln[:], ACT.Exp, scale=-1.0).then_inc(dt_act, 1)

            def keep_b():
                for g in range(GROUPS):
                    b = 2 + 3 * (g % 2)
                    act.wait_ge(b_turned, g + 1)
                    act.activation(Btm[:, g, 0:NC, :], bank[b][:, :].rearrange("p (c n) -> p c n", c=NC),
                                   ACT.Copy).then_inc(b_kept, 1)
                    act.activation(Btm[0:S, g, NC, :], bank[b + 1][0:S, 0:P], ACT.Copy).then_inc(b_kept, 1)

            def exponentials(p, first):
                act.wait_ge(seg_ready, p + 1)
                if not first:
                    act.wait_ge(ssd_done, p)
                if not first:
                    act.wait_ge(y_step, 5 * p - 2)
                for h in range(2):
                    act.activation(E[:, h, 0:SEQ], bank[2 + h][:, :], ACT.Exp).then_inc(decay_ready, 1)
                act.activation(E[0:S, :, SEQ:T + 1],
                               bank[6][0:S, 0:2 * (S + 1)].rearrange("p (h t) -> p h t", h=2),
                               ACT.Exp).then_inc(decay_ready, 1)
                act.activation(E2[:, 0:SEQ], bank[4][:, :], ACT.Exp).then_inc(decay_ready, 1)
                act.activation(E2[:, SEQ:T], bank[6][:, 144:144 + S], ACT.Exp).then_inc(decay_ready, 1)

            def heads():
                n = PLAN["xz"]

                def body(p, first=False, more=True, stats=None):
                    exponentials(p, first)
                    if more:
                        split_hi(n + 3, 2 * p)
                    if stats is not None:
                        group_std(stats)
                    act.wait_ge(h_turned, p + 1)
                    act.activation(hT[:], bank[5][:, 0:(NC - 1) * P].rearrange("p (c n) -> p c n", c=NC - 1),
                                   ACT.Copy).then_inc(hT_ready, 1)
                    if more:
                        if not first:
                            act.wait_ge(z_ready, p)
                            act.wait_ge(gsum_step, p)
                        conv_act(p + 1 + 2 * GROUPS)
                    split_hi(n + 4 if more else n + 3, 2 * p)
                    act.wait_ge(evicted, TILE["xz"] + 2 * p + (5 if more else 4))
                    act.wait_ge(conv_done, 2 * ((p + 1 if more else p) + 2 * GROUPS) + 2)
                    act.activation(th[:, 0:T], yall[:, p, :], ACT.Tanh).then_inc(z_tanh, 1)

                split_hi(n + 2, 0)
                keep_b()
                conv_act(2 * GROUPS)
                body(0, first=True)
                with act.Fori(1, NX - GROUPS) as p:
                    body(p)
                with act.Fori(0, GROUPS - 1) as q:
                    body(q + 12, stats=q)
                body(NX - 1, more=False)

            def group_std(g):
                act.wait_ge(gvar, g + 1)
                act.activation(gsum[:, g, :], gsum[:, g, :], ACT.Sqrt).then_inc(gstd, 1)

            def mixer_out(gain):
                n = PLAN["out"]
                act.wait_ge(ssd_done, NX)
                for p in range(NX):
                    if p == 12:
                        split_hi(n + 2, 0)
                        group_std(GROUPS - 1)
                    act.wait_ge(yn_ready, p + 1)
                    act.activation(yhi[:, p, :], yall[:, p, :], ACT.Copy, scale=column(G_GATE, p)).then_inc(y_hi, 1)
                split_hi(n + 3, 0)
                residual("out", 2, gain, kwise=True)

            def key_value(gain):
                n = PLAN["kv"]
                std(NORM["kv"])
                for c in range(4):
                    split_hi(n + c + 2, 0)
                for k in range(NK):
                    if k < NK - 1:
                        act.wait_ge(xg_used, k + 1)
                    else:
                        act.wait_ge(units_done, n + 4)
                    gained(k, gain)

            def attention():
                n, m = PLAN["q"], TILE["q"]

                def copy_probs(j):
                    for h in range(2):
                        b = 6 if h == 0 else 4
                        act.wait_ge(p_turned, 2 * j + h + 1)
                        act.wait_ge(pv_done, j)
                        act.activation(PT[:, h, :, :].rearrange("p t q -> p (t q)"),
                                       psum[:, b:b + 2, :].rearrange("p b n -> p (b n)")[:, 0:(2 * NC - 1) * P],
                                       ACT.Copy).then_inc(pt_ready, 1)

                def exponentials(g, kp):
                    for h in range(2):
                        hh = 4 * g + 2 * kp + h
                        act.wait_ge(soft, 4 * hh + 4)
                        for c in range(NC):
                            act.activation(probs[:, h, 2 * L * c:2 * L * (c + 1)], sc[:, h, 2 * L * c:2 * L * (c + 1)],
                                           ACT.Exp, bias=nmax[:, h, c:c + 1],
                                           accum_out=rsum[:, h, c:c + 1]).then_inc(p_exp, 1)
                        head = g + 8 * kp + 4 * h
                        act.activation(esink[:, h, :], nmax[:, h, :], ACT.Exp,
                                       bias=acol(SINK, head)).then_inc(p_exp, 1)

                def out_hi(j):
                    act.wait_ge(pv_done, j + 1)
                    act.activation(ohi[:, j, 0:SEQ], bank[6][:, :], ACT.Copy).then_inc(o_hi, 1)

                def body(g, kp, first=False):
                    j = 2 * g + kp
                    if first:
                        std(NORM["q"])
                    split_hi(n + 2 + kp, 2 * g)
                    if first:
                        act.wait_ge(kv_turned, 1)
                        act.activation(VT[:].rearrange("p b v -> p (b v)").rearrange("p (a n) -> p a n", a=2), psum[:, 2:4, :],
                                       ACT.Copy).then_inc(kv_kept, 1)
                        act.activation(Kwin[:], bank[6][:, 0:2 * P], ACT.Copy).then_inc(kv_kept, 1)
                        act.activation(kvsam[:], bank[7][0:S, :], ACT.Copy).then_inc(kv_kept, 1)
                    act.wait_ge(evicted, m + j + 3)
                    for h in range(2):
                        act.activation(Qsam[:, 2 * kp + h, :, g, :],
                                       qs[HD * h:HD * (h + 1), SEQ:T].rearrange("p (b t) -> p b t", b=DEC_BATCH),
                                       ACT.Copy).then_inc(qsam_ready, 1)
                    if not first:
                        copy_probs(j - 1)
                    exponentials(g, kp)
                    if not first:
                        out_hi(j - 1)

                body(0, 0, first=True)
                body(0, 1)
                with act.Fori(1, QH // KVH) as g:
                    body(g, 0)
                    body(g, 1)
                copy_probs(NK - 1)
                sample_exponentials()
                out_hi(NK - 1)

            def sample_exponentials():
                act.wait_ge(ssoft, 5)
                for b in range(DEC_BATCH):
                    act.activation(psam[:, b, :], ssam[:, b, :], ACT.Exp, bias=snmax[:, b:b + 1],
                                   accum_out=srsum[:, b:b + 1]).then_inc(sp_exp, 1)
                act.activation(sesink[:], snmax[:], ACT.Exp, bias=acol(SINK_S, 0)).then_inc(sp_exp, 1)

            def sample_attention():
                act.wait_ge(sp_turned, 1)
                act.activation(PTs[:].rearrange("p b r -> p (b r)").rearrange("p (a n) -> p a n", a=2), psum[:, 5:7, :],
                               ACT.Copy).then_inc(spt_ready, 1)
                for i, b in enumerate((7, 2)):
                    act.activation(PTn[:, 4 * i:4 * i + 4, :].rearrange("p b r -> p (b r)"), bank[b][0:DEC_SEQ, :],
                                   ACT.Copy).then_inc(spt_ready, 1)
                act.wait_ge(spv_done, 1)
                for kp in range(2):
                    for h in range(2):
                        rows = slice(HD * h, HD * (h + 1))
                        act.activation(ohi[rows, kp:NK:2, SEQ:T].rearrange("p g (b t) -> p g b t", b=DEC_BATCH),
                                       sample_out(kp, h), ACT.Copy).then_inc(o_hi, 1)

            act.wait_ge(prm_loaded, 16)
            split_hi(0, 0)
            for k in range(NK):
                act.wait_ge(x_loaded[k], 16)
                gained(k, G_FFN1)
                if k == 0:
                    act.activation(sqsum[:], x[:, 0, :], ACT.Square).then_inc(sumsq, 1)
                else:
                    act.activation(firstsq[:, k - 1, :], x[:, k, :], ACT.Square).then_inc(squared, 1)
                if k == 1:
                    split_hi(1, 0)
            act.wait_ge(c_loaded, 16)
            act.activation(strict_r[:], strict, ACT.Copy).then_inc(consts_r, 1)
            gate_up("gu0", 0)
            residual("down0", 3, G_MIX)
            b_and_c()
            heads()
            mixer_out(G_FFN2)
            gate_up("gu1", 1)
            residual("down1", 3, G_KV)
            key_value(G_FFN1 + NK)
            gate_up("gu2", 2, with_norm=False)
            residual("down2", 3, G_MIX + NK)
            attention()
            sample_attention()
            residual("o", 1, G_FFN2 + NK)
            gate_up("gu3", 3)
            residual("down3", 3, None, last=True)
            act.wait_ge(evicted, TILE["down3"] + NK + 2)
            act.wait_ge(sumsq, NK * NORM["final"] + NK - 1)
            act.activation(sq, x[:, NK - 1, :], ACT.Square).then_inc(last_square, 1)
            std(NORM["final"])
            for k in range(NK):
                act.activation(ybuf[:, k, :], x[:, k, :], ACT.Copy,
                               scale=prm[:, G_FINAL + k:G_FINAL + k + 1]).then_inc(y_gained, 1)

        @block.vector
        def _(dve):
            dve.sem_inc(evicted, 2)

            def split_lo(n, step):
                dve.wait_ge(weights_hi, n + step + 1)
                dve.tensor_tensor(wlo[n % 2][:], wraw[n % 2][:], whi[n % 2][:].bitcast(F32),
                                  ALU.subtract).then_inc(weights_lo, 1)

            def gained_lo(k, gain, q):
                dve.wait_ge(xg_hi, NK * q + k + 1)
                g = prm[:, gain + k:gain + k + 1] if isinstance(k, int) else prm[:, bass.ds(k + gain, 1)]
                dve.scalar_tensor_tensor(xlo[:, k, :], x[:, k, :], g, xhi[:, k, :].bitcast(F32),
                                         ALU.mult, ALU.subtract).then_inc(xg_lo, 1)

            def rms(e):
                dve.wait_ge(norm_sum, e + 1)
                dve.tensor_scalar(halves(rstd[:]), nrm[:, :, 0:HALF], 1.0 / D_MODEL, EPS, ALU.mult,
                                  ALU.add).then_inc(var_ready, 1)
                dve.wait_ge(std_ready, e + 1)
                dve.reciprocal(rstd[:], rstd[:]).then_inc(rstd_ready, 1)
                dve.wait_ge(rstd_ready, e + 1)

            def hidden_lo(before, i):
                dve.wait_ge(h_hi, NF * before + i + 1)
                dve.tensor_tensor(hlo[:, i, :], hidden[:], hhi[:, i, :].bitcast(F32),
                                  ALU.subtract).then_inc(h_lo, 1)

            def gate_up(ph, before, with_norm=True):
                n, m = PLAN[ph], TILE[ph]

                def body(i, first=False):
                    if first and with_norm:
                        rms(NORM[ph])
                    else:
                        split_lo(n + 2, 2 * i)
                    dve.wait_ge(units_done, n + 2 * i + 1)
                    if before or not first:
                        dve.wait_ge(silu_ready, NF * before + i)
                    dve.tensor_tensor(halves(gate[:]), out_of(m % 2), halves(rstd[:]), ALU.mult).then_inc(evicted, 1)
                    if first and with_norm:
                        split_lo(n + 2, 2 * i)
                    if not first:
                        hidden_lo(before, i - 1)
                    split_lo(n + 3, 2 * i)
                    dve.wait_ge(units_done, n + 2 * i + 2)
                    dve.tensor_tensor(halves(up[:]), out_of((m + 1) % 2), halves(rstd[:]), ALU.mult).then_inc(evicted, 1)
                    dve.wait_ge(silu_ready, NF * before + i + 1)
                    dve.wait_ge(evicted, m + 2 * i + 4)
                    dve.tensor_tensor(hidden[:], silu[:], up[:], ALU.mult).then_inc(h_ready, 1)
                body(0, True)
                with dve.Fori(1, NF) as i:
                    body(i)
                hidden_lo(before, NF - 1)

            def residual(ph, per, gain, q, scale=None, last=False, kwise=False):
                n, m = PLAN[ph], TILE[ph]

                def body(i, first=False, splits=2 * per, skip=0):
                    for d in range(2):
                        for a in range(per - 1):
                            if skip <= per * d + a < splits:
                                split_lo(n + 2 + per * d + a, 2 * per * i)
                            if a == 0 and not (first and d == 0) and gain is not None:
                                gained_lo(2 * i + d - 1, gain, q)
                        dve.wait_ge(units_done, n + 2 * per - 1 + d if first and kwise
                                    else n + 2 * per * i + per * d + per)
                        tile = halves(x[:, 2 * i + d, :])
                        if scale is None:
                            dve.tensor_tensor(tile, out_of((m + d) % 2), tile, ALU.add).then_inc(evicted, 1)
                        else:
                            dve.scalar_tensor_tensor(tile, out_of((m + d) % 2), scale, tile, ALU.mult,
                                                     ALU.add).then_inc(evicted, 1)
                        if skip <= per * d + per - 1 < splits:
                            split_lo(n + 2 + per * d + per - 1, 2 * per * i)
                        if per == 1 and not (first and d == 0) and gain is not None:
                            gained_lo(2 * i + d - 1, gain, q)
                body(0, True, skip=2 if kwise else 0)
                with dve.Fori(1, NK // 2 - 1) as i:
                    body(i)
                body(NK // 2 - 1, splits=2 * per - 2 if last else 2 * per)
                if gain is not None:
                    gained_lo(NK - 1, gain, q)


            def seq_rows(buf):
                return buf[:, 3 + SEQ:CBUF].rearrange("p (b r) -> p b r", b=DEC_BATCH)[:, :, 0:DEC_SEQ]

            def conv_in(c, ci, pair, last_inc=evicted):
                dve.wait_ge(conv_saved, 2 * ci)
                seqs = cbuf[:, 3 + SEQ:CBUF].rearrange("p (b r) -> p b r", b=DEC_BATCH)
                dve.tensor_copy(seqs[:, :, 0:3], cstate[:, c, :, :])
                dve.tensor_tensor(cbuf[:, 3:3 + HALF], acc[:, 2 * pair, 0:HALF], rstd[:, 0:HALF], ALU.mult)
                dve.tensor_tensor(cbuf[:, 3 + HALF:3 + SEQ], acc[:, 2 * pair + 1, 0:SEQ - HALF], rstd[:, HALF:SEQ],
                                  ALU.mult)
                dve.tensor_tensor(seqs[:, :, 3:3 + DEC_SEQ],
                                  acc[:, 2 * pair + 1, SEQ - HALF:HALF].rearrange("p (b t) -> p b t", b=DEC_BATCH),
                                  rstd[:, SEQ:T].rearrange("p (b t) -> p b t", b=DEC_BATCH), ALU.mult).then_inc(evicted, 1)

            def conv_taps(c, ci, tile, on_act=False, cacc=cacc):
                dve.wait_ge(evicted, tile + 3)
                if not on_act:
                    dve.tensor_scalar(cacc[:, 0:CLEN], cbuf[:, 0:CLEN], column(G_CONVW, c, CONV), column(G_CONVB, c), ALU.mult,
                                      ALU.add).then_inc(conv_step, 1)
                for tap in range(1, CONV):
                    dve.wait_ge(conv_step, 4 * ci + tap)
                    dve.scalar_tensor_tensor(cacc[:, 0:CLEN], cbuf[:, tap:tap + CLEN], column(G_CONVW + tap, c, CONV), cacc[:, 0:CLEN],
                                             ALU.mult, ALU.add).then_inc(conv_step, 1)

            def conv_out(out, ci, cacc=cacc):
                dve.wait_ge(conv_tanh, ci + 1)
                dve.scalar_tensor_tensor(out[:, 0:SEQ], th[:, 0:SEQ], 1.0, cacc[:, 0:SEQ], ALU.add,
                                         ALU.mult).then_inc(conv_done, 1)
                dve.scalar_tensor_tensor(out[:, SEQ:T].rearrange("p (b t) -> p b t", b=DEC_BATCH), seq_rows(th), 1.0,
                                         seq_rows(cacc), ALU.add, ALU.mult).then_inc(conv_done, 1)

            def b_c_out(c):
                conv_out(BT[:, c, :] if c < GROUPS else CT[:, c - GROUPS, :], c, (cacc, cacc2)[c % 2])

            def b_and_c():
                n, m = PLAN["bc"], TILE["bc"]
                rms(NORM["dt"])
                evict_dt()
                split_lo(PLAN["dt"] + 2, 0)
                for c in range(2 * GROUPS):
                    if c == 0:
                        dve.wait_ge(st_loaded, 32)
                        dve.wait_ge(cleared, 5)
                        dve.wait_ge(conv_prm, 1)
                    dve.wait_ge(units_done, n + c + 1)
                    if c:
                        dve.wait_ge(conv_step, 4 * c)
                    conv_in(NX + c, c, (c + 1) % 2)
                    if c:
                        b_c_out(c - 1)
                    else:
                        split_lo(n + 2, 0)
                    conv_taps(NX + c, c, m + c, on_act=True, cacc=(cacc, cacc2)[c % 2])
                    if c in (1, 5):
                        softplus(c // 5)

            def evict_dt():
                dve.wait_ge(units_done, PLAN["dt"] + 1)
                dve.tensor_tensor(halves(dts[0][:]), psum[0:HEADS, 0:2, 0:HALF],
                                  halves(rstd[0:HEADS, :]), ALU.mult).then_inc(evicted, 1)

            def softplus(part):
                s1, e, u, ln, r = dts
                if part == 0:
                    dve.wait_ge(evicted, TILE["dt"] + 3)
                    dve.wait_ge(dt_act, 3)
                    dve.tensor_scalar(s1[:], s1[:], dtprm[:, 0:1], 0.0, ALU.add, ALU.max).then_inc(dt_dve, 1)
                    dve.tensor_scalar(u[:], e[:], 1.0, None, ALU.add).then_inc(dt_dve, 1)
                    dve.wait_ge(dt_dve, 2)
                    dve.scalar_tensor_tensor(e[:], u[:], -1.0, e[:], ALU.add, ALU.subtract).then_inc(dt_dve, 1)
                    return
                dve.wait_ge(dt_act, 5)
                dve.wait_ge(dt_dve, 3)
                dve.tensor_tensor(e[:], e[:], r[:], ALU.mult).then_inc(dt_dve, 1)
                dve.tensor_tensor(s1[:], s1[:], ln[:], ALU.add).then_inc(dt_dve, 1)
                dve.wait_ge(dt_dve, 5)
                dve.tensor_tensor(dtp[0:HEADS, :], s1[:], e[:], ALU.subtract).then_inc(dt_dve, 1)
                dve.wait_ge(dt_dve, 6)
                dve.tensor_scalar(dtp[HEADS:2 * HEADS, :], dtp[0:HEADS, :], dtprm[:, 2:3], -1.0, ALU.mult,
                                  ALU.mult).then_inc(dt_dve, 1)

            def keep_dt():
                dve.wait_ge(dt_turned, 1)
                turned = bank[7][:, 0:256].rearrange("p (c h) -> p c h", c=NC)
                dve.tensor_copy(dT[:, 0:NC, 0:HEADS], turned[:, :, 0:HEADS]).then_inc(dt_kept, 1)
                dve.tensor_copy(dT[0:S, NC, :], bank[7][0:S, 256:320]).then_inc(dt_kept, 1)
                dve.tensor_copy(dahi, turned[:, :, HEADS:]).then_inc(dt_kept, 1)
                dve.wait_ge(dt_kept, 3)
                dve.tensor_tensor(dalo[:], turned[:, :, HEADS:], dahi.bitcast(F32), ALU.subtract).then_inc(dt_kept, 1)
                dve.wait_ge(dt_kept, 4)

            def mask_cb():
                for g in range(GROUPS):
                    b = 2 + 3 * (g % 2)
                    dve.wait_ge(cb_done, g + 1)
                    dve.tensor_tensor(cbm[:, g, 0:SEQ].rearrange("p (c t) -> p c t", c=NC),
                                      bank[b + 2][:, :].rearrange("p (c t) -> p c t", c=NC),
                                      tri.unsqueeze(1).to_broadcast([P, NC, L]), ALU.mult).then_inc(cb_kept, 1)
                    dve.tensor_tensor(cbm[0:S, g, SEQ:T], bank[b + 1][0:S, P:P + S], tri_s[:, 0:S],
                                      ALU.mult).then_inc(cb_kept, 1)

            def heads():
                n, m = PLAN["xz"], TILE["xz"]

                def by_head(buf):
                    return buf.rearrange("p c (h d) -> p c h d", h=2)

                def weighted(p, first, finish):
                    dve.wait_ge(x_turned, p + 1)
                    if not first:
                        dve.wait_ge(ssd_done, p)
                    dt = dT[:, :, 0:HEADS].rearrange("p c (j h) -> p c j h", h=2)[:, :, p, :]
                    dve.tensor_tensor(by_head(xdt[:, 0:NC, :]), bank[5][:, :].rearrange("p (c h d) -> p c h d", c=NC, h=2),
                                      dt[:, 0:NC, :].unsqueeze(3).to_broadcast([P, NC, 2, HEAD_DIM]),
                                      ALU.mult).then_inc(xdt_ready, 1)
                    dve.tensor_tensor(xdt[0:S, NC, :].rearrange("p (h d) -> p h d", h=2),
                                      bank[7][0:S, 0:P].rearrange("p (h d) -> p h d", h=2),
                                      dt[0:S, NC, :].unsqueeze(2).to_broadcast([S, 2, HEAD_DIM]),
                                      ALU.mult).then_inc(xdt_ready, 1)
                    if finish is not None:
                        group_rstd(finish)
                    dve.wait_ge(decay_ready, 5 * p + 3)
                    dve.wait_ge(xdt_ready, 2 * p + 2)
                    to_end = E[:, :, L - 1:SEQ:L].rearrange("p h c -> p c h")
                    dve.tensor_tensor(by_head(xdd[:, 0:NC, :]), by_head(xdt[:, 0:NC, :]),
                                      to_end.unsqueeze(3).to_broadcast([P, NC, 2, HEAD_DIM]), ALU.mult).then_inc(xdd_ready, 1)
                    dve.tensor_tensor(xdd[0:S, NC, :].rearrange("p (h d) -> p h d", h=2),
                                      xdt[0:S, NC, :].rearrange("p (h d) -> p h d", h=2),
                                      E[0:S, :, T:T + 1].to_broadcast([S, 2, HEAD_DIM]), ALU.mult).then_inc(xdd_ready, 1)

                def chain(p, first):
                    dve.wait_ge(s_ready, p + 1)
                    if not first:
                        dve.wait_ge(hp_stored, 16 * p)
                    dve.tensor_copy(hst[:, 0, :], bank[2][:, 0:P]).then_inc(h_step, 1)
                    for c in range(1, NC):
                        dve.wait_ge(h_step, 4 * p + c)
                        dve.scalar_tensor_tensor(hst[:, c, :], hst[:, c - 1, :], E2[:, c * L + L - 1:c * L + L],
                                                 bank[2][:, c * P:(c + 1) * P], ALU.mult, ALU.add).then_inc(h_step, 1)

                def gated(p):
                    dve.wait_ge(ssd_done, p + 1)
                    dve.wait_ge(skip_ready, p + 1)
                    dve.tensor_tensor(yd[:, 0:SEQ], yd[:, 0:SEQ], bank[7][:, :], ALU.add).then_inc(y_step, 1)
                    dve.tensor_tensor(yd[:, SEQ:T], yd[:, SEQ:T], bank[6][:, 448:512], ALU.add).then_inc(y_step, 1)
                    dve.tensor_tensor(yo[:, L:T], bank[6][:, 0:448], E2[:, L:T], ALU.mult).then_inc(y_step, 1)
                    dve.wait_ge(y_step, 5 * p + 3)
                    dve.tensor_tensor(yd[:, L:T], yd[:, L:T], yo[:, L:T], ALU.add).then_inc(y_step, 1)
                    dve.wait_ge(z_tanh, p + 1)
                    dve.scalar_tensor_tensor(yall[:, p, :], th[:, 0:T], 1.0, yall[:, p, :], ALU.add,
                                             ALU.mult).then_inc(z_ready, 1)
                    dve.wait_ge(y_step, 5 * p + 4)
                    dve.wait_ge(z_ready, p + 1)
                    dve.tensor_tensor(yall[:, p, :], yd[:], yall[:, p, :], ALU.mult).then_inc(y_step, 1)

                def body(p, g, first=False, more=True, stats=None, finish=None):
                    j = p + 1
                    weighted(p, first, finish)
                    if more:
                        dve.wait_ge(units_done, n + 2 * p + 2)
                        conv_in(j, j + 2 * GROUPS, 0)
                        split_lo(n + 3, 2 * p)
                    if stats is not None:
                        group_var(stats, 0)
                    dve.wait_ge(xdd_ready, 2 * p + 2)
                    dve.tensor_tensor(E[:, :, 0:T], E[:, :, 0:T], cbm[:, g, :].unsqueeze(1).to_broadcast([P, 2, T]),
                                      ALU.mult).then_inc(m_ready, 1)
                    chain(p, first)
                    if more:
                        conv_taps(j, j + 2 * GROUPS, m + 2 * p + 1)
                    dve.wait_ge(ss_ready, p + 1)
                    dve.wait_ge(h0_decayed, p + 1)
                    dve.tensor_tensor(h0s[:].rearrange("p b n -> p (b n)").rearrange("p (a n) -> p a n", a=2), psum[:, 3:5, :],
                                      h0s[:].rearrange("p b n -> p (b n)").rearrange("p (a n) -> p a n", a=2),
                                      ALU.add).then_inc(ss_final, 1)
                    if more:
                        dve.wait_ge(x_turned, j)
                        dve.wait_ge(skip_ready, j)
                        conv_out(xs, j + 2 * GROUPS)
                    dve.wait_ge(units_done, n + 2 * p + (3 if more else 2))
                    dve.scalar_tensor_tensor(halves(yall[:, p, :]), out_of(0), 0.5, halves(rstd[:]), ALU.mult,
                                             ALU.mult).then_inc(evicted, 1)
                    gated(p)
                    if more:
                        split_lo(n + 4, 2 * p)

                b_c_out(2 * GROUPS - 1)
                dve.sem_inc(evicted, 1)
                dve.wait_ge(units_done, n + 1)
                conv_in(0, 2 * GROUPS, 1)
                keep_dt()
                mask_cb()
                conv_taps(0, 2 * GROUPS, m)
                dve.wait_ge(weights_lo, n + 2)
                split_lo(n + 2, 0)
                conv_out(xs, 2 * GROUPS)
                body(0, 0, first=True)
                with dve.Fori(1, 4) as p:
                    body(p, 0)
                with dve.Fori(1, GROUPS - 1) as g:
                    with dve.Fori(0, 4) as q:
                        body(g * 4 + q, g)
                body(12, GROUPS - 1, stats=0)
                with dve.Fori(1, GROUPS - 1) as q:
                    body(q + 12, GROUPS - 1, stats=q, finish=q - 1)
                body(NX - 1, GROUPS - 1, more=False, finish=GROUPS - 2)

            def group_var(g, b):
                dve.wait_ge(gnorm_sum, g + 1)
                dve.tensor_scalar(halves(gsum[:, g, :]), psum[:, b:b + 2, 0:HALF], float(GROUPS) / D_INNER, EPS,
                                  ALU.mult, ALU.add).then_inc(gvar, 1)

            def group_rstd(g):
                dve.wait_ge(gstd, g + 1)
                dve.reciprocal(gsum[:, g, :], gsum[:, g, :]).then_inc(grstd, 1)

            def group_norm(g):
                group_rstd(g)
                dve.wait_ge(grstd, g + 1)
                dve.wait_ge(yn_ready, 4 * g)
                for p in range(4 * g, 4 * g + 4):
                    dve.tensor_tensor(yall[:, p, :], yall[:, p, :], gsum[:, g, :], ALU.mult).then_inc(yn_ready, 1)

            def mixer_out(gain, q):
                n = PLAN["out"]
                for p in range(NX):
                    if p == 4:
                        split_lo(n + 1, 0)
                    if p == 12:
                        group_var(GROUPS - 1, 6)
                        split_lo(n + 2, 0)
                        group_norm(GROUPS - 1)
                    low_part(p)
                split_lo(n + 3, 0)
                residual("out", 2, gain, q, kwise=True)

            def low_part(p):
                dve.wait_ge(y_hi, p + 1)
                dve.scalar_tensor_tensor(ylo[:, p, :], yall[:, p, :], column(G_GATE, p), yhi[:, p, :].bitcast(F32),
                                         ALU.mult, ALU.subtract).then_inc(y_lo, 1)

            def key_value(gain, q):
                n, m = PLAN["kv"], TILE["kv"]
                rms(NORM["kv"])
                for c in range(4):
                    dve.wait_ge(units_done, n + c + 1)
                    dve.tensor_tensor(halves(KVT[:, c, :]), out_of((m + c) % 2), halves(rstd[:]), ALU.mult).then_inc(evicted, 1)
                    split_lo(n + c + 2, 0)
                for k in range(NK):
                    gained_lo(k, gain, q)

            def attention():
                n, m = PLAN["q"], TILE["q"]

                def softmax_in(g, kp):
                    for h in range(2):
                        hh = 4 * g + 2 * kp + h
                        head = g + 8 * kp + 4 * h
                        dve.wait_ge(scores_done, hh + 1)
                        flat = psum[:, 2 + 2 * h:4 + 2 * h, :].rearrange("p b n -> p (b n)")
                        by_block = lambda v: v.rearrange("p (c k) -> p c k", k=2 * L)
                        dve.scalar_tensor_tensor(by_block(sc[:, h, 2 * L:]),
                                                 negd[:].unsqueeze(1).to_broadcast([P, NC - 1, 2 * L]), acol(SLOPE, head),
                                                 by_block(flat[:, 2 * L:]), ALU.mult, ALU.add).then_inc(soft, 1)
                        dve.scalar_tensor_tensor(sc[:, h, L:2 * L], negd[:, L:2 * L], acol(SLOPE, head), flat[:, L:2 * L],
                                                 ALU.mult, ALU.add).then_inc(soft, 1)
                        dve.wait_ge(soft, 4 * hh + 2)
                        dve.tensor_reduce(nmax[:, h, :], by_block(sc[:, h, :]), mybir.AxisListType.X, ALU.max).then_inc(soft, 1)
                        dve.wait_ge(soft, 4 * hh + 3)
                        dve.tensor_scalar(nmax[:, h, :], nmax[:, h, :], acol(SINK, head), -1.0, ALU.max,
                                          ALU.mult).then_inc(soft, 1)

                def denominators(j):
                    for h in range(2):
                        hh = 2 * j + h
                        dve.wait_ge(p_exp, 5 * hh + 5)
                        dve.tensor_tensor(rsum[:, h, :], rsum[:, h, :], esink[:, h, :], ALU.add).then_inc(den, 1)
                        dve.wait_ge(den, 2 * hh + 1)
                        dve.wait_ge(p_ready, 2 * j)
                        dve.reciprocal(rden[:, h, :], rsum[:, h, :]).then_inc(den, 1)

                def out_lo(j):
                    dve.wait_ge(o_hi, j + 1)
                    dve.tensor_tensor(olo[:, j, 0:SEQ], bank[6][:, :], ohi[:, j, 0:SEQ].bitcast(F32),
                                      ALU.subtract).then_inc(o_lo, 1)

                def body(g, kp, first=False):
                    j = 2 * g + kp
                    if first:
                        rms(NORM["q"])
                    dve.wait_ge(units_done, n + j + 1)
                    if not first:
                        dve.wait_ge(scores_done, 2 * j)
                        dve.wait_ge(qsam_ready, 2 * j)
                    dve.scalar_tensor_tensor(halves(qs[:]), out_of(0), HD ** -0.5, halves(rstd[:]), ALU.mult,
                                             ALU.mult).then_inc(evicted, 1)
                    split_lo(n + 2 + kp, 2 * g)
                    softmax_in(g, kp)
                    denominators(j)
                    if not first:
                        out_lo(j - 1)

                dve.wait_ge(att_cleared, 1)
                dve.wait_ge(att_loaded, 16)
                body(0, 0, first=True)
                body(0, 1)
                with dve.Fori(1, QH // KVH) as g:
                    body(g, 0)
                    body(g, 1)
                sample_softmax()
                out_lo(NK - 1)

            def sample_softmax():
                dve.wait_ge(ssc_done, 1)
                for i, (b0, nb) in enumerate(((0, 3), (3, 3), (6, 2))):
                    dve.tensor_tensor(ssam[:, b0:b0 + nb, :], bank[i][:, 0:nb * KS].rearrange("p (b k) -> p b k", b=nb),
                                      attc[:, BIAS_S:BIAS_S + KS].unsqueeze(1).to_broadcast([P, nb, KS]),
                                      ALU.add).then_inc(ssoft, 1)
                dve.wait_ge(ssoft, 3)
                dve.tensor_reduce(snmax[:], ssam[:], mybir.AxisListType.X, ALU.max).then_inc(ssoft, 1)
                dve.wait_ge(ssoft, 4)
                dve.tensor_scalar(snmax[:], snmax[:], acol(SINK_S, 0), -1.0, ALU.max, ALU.mult).then_inc(ssoft, 1)
                dve.wait_ge(sp_exp, DEC_BATCH + 1)
                dve.tensor_tensor(srsum[:], srsum[:], sesink[:], ALU.add).then_inc(sden, 1)
                dve.wait_ge(sden, 1)
                dve.reciprocal(srden[:], srsum[:]).then_inc(sden, 1)
                dve.wait_ge(sden, 2)
                dve.tensor_tensor(psam[:], psam[:], srden[:].unsqueeze(2).to_broadcast([P, DEC_BATCH, KS]),
                                  ALU.mult).then_inc(sp_ready, 1)

            def sample_attention():
                dve.wait_ge(o_hi, NK + 4)
                for kp in range(2):
                    for h in range(2):
                        rows = slice(HD * h, HD * (h + 1))
                        dve.tensor_tensor(olo[rows, kp:NK:2, SEQ:T].rearrange("p g (b t) -> p g b t", b=DEC_BATCH),
                                          sample_out(kp, h),
                                          ohi[rows, kp:NK:2, SEQ:T].bitcast(F32).rearrange("p g (b t) -> p g b t", b=DEC_BATCH),
                                          ALU.subtract).then_inc(o_lo, 1)

            dve.wait_ge(prm_loaded, 16)
            conv_params = prm[:, G_CONVB:NPARAM]
            dve.tensor_scalar(conv_params, conv_params, 0.5, None, ALU.mult).then_inc(conv_prm, 1)
            split_lo(0, 0)
            for k in range(NK):
                gained_lo(k, G_FFN1, 0)
                if k == 1:
                    split_lo(1, 0)
            gate_up("gu0", 0)
            residual("down0", 3, G_MIX, 1, 0.5)
            b_and_c()
            heads()
            mixer_out(G_FFN2, 2)
            gate_up("gu1", 1)
            residual("down1", 3, G_KV, 3, 0.5)
            key_value(G_FFN1 + NK, 4)
            gate_up("gu2", 2, with_norm=False)
            residual("down2", 3, G_MIX + NK, 5, 0.5)
            attention()
            sample_attention()
            residual("o", 1, G_FFN2 + NK, 6)
            gate_up("gu3", 3)
            residual("down3", 3, None, None, 0.5, last=True)
            rms(NORM["final"])
            for k in range(NK_DVE):
                dve.wait_ge(y_gained, k + 1)
                dve.tensor_tensor(ybuf[:, k, :], ybuf[:, k, :], rstd[:], ALU.mult).then_inc(y_ready, 1)

        @block.gpsimd
        def _(pool):
            def squares(e, first_tile, tiles=NK):
                def body(k, first=False):
                    pool.wait_ge(evicted, first_tile + k + 3)
                    if first:
                        pool.tensor_tensor(sqsum[:], x[:, 0, :], x[:, 0, :], ALU.mult).then_inc(sumsq, 1)
                        return
                    pool.wait_ge(sumsq, NK * e + k)
                    pool.tensor_tensor(sq, x[:, k, :], x[:, k, :], ALU.mult).then_inc(squared, 1)
                    pool.wait_ge(squared, (NK - 1) * e + k)
                    pool.tensor_tensor(sqsum[:], sqsum[:], sq, ALU.add).then_inc(sumsq, 1)
                body(0, True)
                with pool.Fori(1, tiles) as k:
                    body(k)

            def load_state(p):
                pool.dma_start(h0s[:], ssm_state[:, p, :, :].rearrange("b q n -> q b n")).then_inc(h0_loaded, 16)

            def load_state_t(p):
                pool.dma_start(h0T[:], ssm_state_t[:, p, :, :]).then_inc(h0t_loaded, 16)

            def prepare_mixer():
                pool.wait_ge(units_done, PLAN["bc"])
                pool.dma_start(cstate[:], conv_state).then_inc(st_loaded, 16)
                pool.dma_start(dtprm[:, 0:2], dt_params).then_inc(st_loaded, 16)
                load_state(0)
                load_state_t(0)
                pool.memset(cbuf[:, 0:3], 0.0).then_inc(cleared, 1)
                pool.memset(cbm[:, :, SEQ:T], 0.0).then_inc(cleared, 1)
                pool.memset(E[:, :, SEQ:T], 0.0).then_inc(cleared, 1)
                pool.memset(dT[:, NC, :], 0.0).then_inc(cleared, 1)
                pool.memset(gsum[:], 0.0).then_inc(cleared, 1)

            def keep_rows(c, ci, tile):
                pool.wait_ge(evicted, tile + 3)
                pool.tensor_copy(cnew[:, c, 0:3], cbuf[:, SEQ:SEQ + 3]).then_inc(conv_saved, 1)
                pool.tensor_copy(cstate[:, c, :, :],
                                 cbuf[:, 3 + SEQ:CBUF].rearrange("p (b r) -> p b r", b=DEC_BATCH)[:, :, DEC_SEQ:DEC_SEQ + 3]
                                 ).then_inc(conv_saved, 1)

            def seg_operands(p):
                for src, seg in ((dahi, seghi), (dalo[:], seglo)):
                    da = src.bitcast(F32).rearrange("p c (j h) -> p c j h", h=2)[:, :, p, :]
                    pool.tensor_tensor(seg[:].rearrange("p h c t -> p c h t"),
                                       tri.unsqueeze(1).unsqueeze(1).to_broadcast([P, NC, 2, L]),
                                       da.unsqueeze(3).to_broadcast([P, NC, 2, L]), ALU.mult).then_inc(seg_lhs, 1)
                dta = dT[:, :, HEADS:2 * HEADS].rearrange("p c (j h) -> p c j h", h=2)[:, :, p, :]
                pool.tensor_tensor(segs[:], tri_s.unsqueeze(1).to_broadcast([S, 2, S + 1]),
                                   dta[0:S, NC, :].unsqueeze(2).to_broadcast([S, 2, S + 1]), ALU.mult).then_inc(seg_lhs, 1)

            def heads():
                m = TILE["xz"]

                def body(p, g, first=False, more=True, finish=None):
                    pool.wait_ge(conv_done, 2 * (2 * GROUPS + p) + 2)
                    if not first:
                        pool.wait_ge(y_step, 5 * p)
                    pool.tensor_tensor(yd[:], xs[:], column(G_D, p).to_broadcast([P, T]), ALU.mult).then_inc(skip_ready, 1)
                    pool.wait_ge(decay_ready, 5 * p + 5)
                    pool.wait_ge(h0_loaded, 16 * p + 16)
                    pool.tensor_tensor(h0s[:], h0s[:],
                                       E2[:, SEQ + DEC_SEQ - 1:T:DEC_SEQ].unsqueeze(2).to_broadcast([P, DEC_BATCH, P]),
                                       ALU.mult).then_inc(h0_decayed, 1)
                    if more:
                        pool.wait_ge(seg_ready, p + 1)
                        seg_operands(p + 1)
                        keep_rows(p + 1, p + 1 + 2 * GROUPS, m + 2 * p + 1)
                    pool.wait_ge(h_step, 4 * p + 4)
                    pool.wait_ge(h_turned, p + 1)
                    pool.wait_ge(ss_final, p + 1)
                    pool.dma_start(ssm_p_out[p], hst[:, NC - 1, :]).then_inc(hp_stored, 16)
                    pool.dma_start(ssm_s_out[:, p, :, :].rearrange("b q n -> q b n"), h0s[:]).then_inc(hs_stored, 16)
                    if more:
                        pool.wait_ge(hs_stored, 16 * p + 16)
                        load_state(p + 1)
                        pool.wait_ge(ssd_done, p + 1)
                        load_state_t(p + 1)
                    if finish is not None:
                        pool.wait_ge(grstd, finish + 1)
                        for i in range(4):
                            pool.tensor_tensor(yall[:, finish * 4 + i, :], yall[:, finish * 4 + i, :],
                                               gsum[:, finish, :], ALU.mult).then_inc(yn_ready, 1)
                    pool.wait_ge(y_step, 5 * p + 5)
                    if not first:
                        pool.wait_ge(gsum_step, p)
                    pool.tensor_tensor(sq, yall[:, p, :], yall[:, p, :], ALU.mult).then_inc(ysq, 1)
                    pool.wait_ge(ysq, p + 1)
                    pool.tensor_tensor(gsum[:, g, :], gsum[:, g, :], sq, ALU.add).then_inc(gsum_step, 1)

                def sequence_b(g, first=False):
                    if not first:
                        pool.wait_ge(ss_ready, 4 * g)
                    pool.tensor_tensor(Bm[:], Btm[0:S, g, NC, :].unsqueeze(1).to_broadcast([S, DEC_BATCH, P]),
                                       in_seq.unsqueeze(2).to_broadcast([S, DEC_BATCH, P]), ALU.mult).then_inc(bm_ready, 1)

                keep_rows(0, 2 * GROUPS, m)
                pool.wait_ge(dt_kept, 4)
                seg_operands(0)
                pool.wait_ge(b_kept, 2 * GROUPS)
                sequence_b(0, first=True)
                body(0, 0, first=True)
                with pool.Fori(1, 4) as p:
                    body(p, 0)
                with pool.Fori(1, GROUPS - 1) as g:
                    sequence_b(g)
                    with pool.Fori(0, 4) as q:
                        body(g * 4 + q, g)
                sequence_b(GROUPS - 1)
                body(12, GROUPS - 1)
                with pool.Fori(1, GROUPS - 1) as q:
                    body(q + 12, GROUPS - 1, finish=q - 1)
                body(NX - 1, GROUPS - 1, more=False, finish=GROUPS - 2)
                pool.wait_ge(conv_saved, 2 * NXBC)
                pool.dma_start(conv_p_out, cnew[:]).then_inc(cnew_stored, 16)
                pool.dma_start(conv_s_out, cstate[:]).then_inc(cnew_stored, 16)
                pool.wait_ge(cnew_stored, 32)
                pool.wait_ge(hp_stored, 16 * NX)
                pool.wait_ge(hs_stored, 16 * NX)

            def prepare_attention():
                pool.wait_ge(units_done, PLAN["q"])
                pool.dma_start(attc[:], att_consts).then_inc(att_loaded, 16)
                pool.memset(sc[:, :, 0:L], MASKED).then_inc(att_cleared, 1)
                pool.dma_start(Ksam[:, :, :, 0:WINDOW], cache_kt).then_inc(kcache_loaded, 16)
                pool.dma_start(Vsam[:], cache_v).then_inc(vsam_loaded, 16)

            def attention():
                pool.wait_ge(kv_kept, 3)
                pool.dma_start(kv_new_out, kvsam[:]).then_inc(new_stored, 16)
                pool.dma_start(kwin_p_out, Kwin[:]).then_inc(win_stored, 16)
                pool.dma_start(vwin_p_out, VT[:, NC - 1, :]).then_inc(win_stored, 16)
                for kv in range(KVH):
                    pool.tensor_copy(Ksam[:, kv, :, WINDOW:KS],
                                     KVT[HD * (kv % 2):HD * (kv % 2 + 1), kv // 2, SEQ:T].rearrange("p (b t) -> p b t", b=DEC_BATCH)
                                     ).then_inc(ksam_ready, 1)
                    pool.wait_ge(ksam_ready, kv + 1)

                def scale(j):
                    for h in range(2):
                        pool.wait_ge(den, 2 * (2 * j + h) + 2)
                        by_block = probs[:, h, :].rearrange("p (c k) -> p c k", c=NC)
                        pool.tensor_tensor(by_block, by_block, rden[:, h, :].unsqueeze(2).to_broadcast([P, NC, 2 * L]),
                                           ALU.mult).then_inc(p_ready, 1)
                with pool.Fori(0, NK) as j:
                    scale(j)
                pool.wait_ge(new_stored, 16)
                pool.wait_ge(units_done, PLAN["o"])
                pool.dma_start(Vnew[:], kv_new_out[:, KVH * HD:].rearrange("(b t) v -> t b v", b=DEC_BATCH)).then_inc(vnew_loaded, 16)
                pool.wait_ge(win_stored, 32)

            pool.memset(ones_r[:].bitcast(F32), 0.0).then_inc(ones_set, 1)
            pool.wait_ge(ones_set, 1)
            pool.memset(ones_r[:, HEAD_DIM:2 * HEAD_DIM].bitcast(F32), 1.0).then_inc(consts_r, 1)
            for k in range(1, NK):
                pool.wait_ge(squared, k)
                pool.wait_ge(sumsq, k)
                pool.tensor_tensor(sqsum[:], sqsum[:], firstsq[:, k - 1, :], ALU.add).then_inc(sumsq, 1)
            squares(1, TILE["down0"])
            pool.dma_start(kv_kept_out, cache_kv[:, :, DEC_SEQ:WINDOW, :]).then_inc(cache_moved, 16)
            prepare_mixer()
            for c in range(2 * GROUPS):
                keep_rows(NX + c, c, TILE["bc"] + c)
                if c:
                    n = PLAN["bc"] + c + 2
                    pool.wait_ge(weights_lo, n)
                    pool.wait_ge(weights_hi, n + 1)
                    pool.tensor_tensor(wlo[n % 2][:], wraw[n % 2][:], whi[n % 2][:].bitcast(F32),
                                       ALU.subtract).then_inc(weights_lo, 1)
            heads()
            squares(2, TILE["out"])
            squares(3, TILE["down1"])
            squares(4, TILE["down2"])
            prepare_attention()
            attention()
            squares(5, TILE["o"])
            squares(6, TILE["down3"], tiles=NK - 1)
            pool.wait_ge(rstd_ready, NORM["final"] + 1)
            pool.wait_ge(y_gained, NK)
            for k in range(NK_DVE, NK):
                pool.tensor_tensor(ybuf[:, k, :], ybuf[:, k, :], rstd[:], ALU.mult).then_inc(y_ready_pool, 1)
            pool.wait_ge(cache_moved, 16)


def units(w):
    K, M = w.shape
    kt = K // P
    kp = -(-kt // UNIT) * UNIT
    out = np.zeros((M // P, kp // UNIT, P, UNIT, P), w.dtype)
    v = w.reshape(kt, P, M // P, P).transpose(2, 1, 0, 3)
    for a in range(kp // UNIT):
        n = min(UNIT, kt - a * UNIT)
        out[:, a, :, :n] = v[:, :, a * UNIT:a * UNIT + n]
    return out.reshape(-1, P, UNIT * P)


def gate_up_units(w):
    u = units(w)
    return np.stack([u[:NF], u[NF:]], 1).reshape(-1, P, UNIT * P)


def columns(v):
    return v.reshape(-1, P).T


def per_feature(v):
    return np.ascontiguousarray(v.T.reshape(-1, P, v.shape[0]).transpose(1, 0, 2))


def kernel(**inputs):
    import concourse.bacc as bacc
    from concourse.bass_utils import run_bass_kernel_spmd

    I = {k: np.asarray(v) for k, v in inputs.items()}
    G = QH // KVH

    w_in = I["ssm_w_in"][0]
    wz, wx, wbc = w_in[:, :D_INNER], w_in[:, D_INNER:2 * D_INNER], w_in[:, 2 * D_INNER:D_INNER + P * NXBC]
    wdt = np.zeros((D_MODEL, P), w_in.dtype)
    wdt[:, :HEADS] = w_in[:, D_INNER + P * NXBC:]
    ux, uz = units(wx), units(wz)
    w_out = units(I["ssm_w_out"][0])
    w_out[1:3] = w_out[2:0:-1].copy()
    by_tile = (KVH // 2, 2, G, HD)
    wq = I["attn_w_q"][0].reshape((D_MODEL,) + by_tile).transpose(0, 3, 1, 2, 4).reshape(D_MODEL, D_MODEL)
    wo = I["attn_w_o"][0].reshape(by_tile + (D_MODEL,)).transpose(2, 0, 1, 3, 4).reshape(D_MODEL, D_MODEL)
    weights = np.concatenate([
        gate_up_units(I["ffn1_w_gu"][0]), units(I["ffn1_w_down"][0]),
        units(wdt), units(wbc), ux[:1], np.stack([ux[1:], uz[:-1]], 1).reshape(-1, P, UNIT * P), uz[-1:], w_out,
        gate_up_units(I["ffn2_w_gu"][0]), units(I["ffn2_w_down"][0]), units(I["w_kv"]),
        gate_up_units(I["ffn1_w_gu"][1]), units(I["ffn1_w_down"][1]), units(wq), units(wo),
        gate_up_units(I["ffn2_w_gu"][1]), units(I["ffn2_w_down"][1])])

    params = np.zeros((P, NPARAM), np.float32)
    for at, v in ((G_FFN1, I["ffn1_norm"]), (G_MIX, I["mix_norm"]), (G_FFN2, I["ffn2_norm"]), (G_KV, I["kv_norm"]),
                  (G_FINAL, I["final_norm"]), (G_GATE, I["ssm_gate_norm"]), (G_D, np.repeat(I["ssm_d"], HEAD_DIM)),
                  (G_CONVB, I["ssm_conv_b"])):
        c = columns(v)
        params[:, at:at + c.shape[1]] = c
    params[:, G_CONVW:] = I["ssm_conv_w"][0].reshape(CONV, NXBC, P).transpose(2, 1, 0).reshape(P, -1)

    consts = np.zeros((P, NCONST), np.float32)
    a, s = np.arange(P), np.arange(S)
    same = s[:, None] // DEC_SEQ == s // DEC_SEQ
    consts[:, C_ONES:C_ONES + P] = 1
    consts[:, C_IDENT:C_IDENT + P] = np.eye(P)
    consts[:, C_TRI:C_TRI + P] = a[:, None] <= a
    consts[:, C_STRICT:C_STRICT + P] = a[:, None] > a
    consts[:S, C_TRI_S:C_TRI_S + S] = same & (s[:, None] <= s)
    consts[:S, C_TRI_S + S] = 1
    consts[:S, C_STRICT_S:C_STRICT_S + S] = same & (s[:, None] > s)
    consts[:S, C_BLOCK:C_BLOCK + DEC_BATCH] = s[:, None] // DEC_SEQ == np.arange(DEC_BATCH)

    att = np.zeros((P, NATT), np.float32)
    slopes = (2.0 ** (-8.0 * np.arange(1, QH + 1) / QH)).astype(np.float32)
    dist = WINDOW + a[:, None] - np.arange(2 * L)
    att[:, NEGD:NEGD + 2 * L] = np.where((dist >= 0) & (dist < WINDOW), -dist, MASKED)
    rows = np.arange(P)
    dist = WINDOW + (rows % DEC_SEQ)[:, None] - np.arange(KS)
    bias = -slopes[rows // DEC_SEQ][:, None] * dist.astype(np.float32)
    att[:, BIAS_S:BIAS_S + KS] = np.where((dist >= 0) & (dist < WINDOW), bias, MASKED)
    att[:, SLOPE:SLOPE + QH] = slopes
    att[:, SINK:SINK + QH] = I["attn_sinks"][0]
    att[:, SINK_S] = np.repeat(I["attn_sinks"][0], DEC_SEQ)

    state = I["state_ssm"][0].reshape(DEC_BATCH, NX, P, D_STATE)
    cache_k, cache_v = I["cache_k_win"], I["cache_v_win"]
    arrays = {
        "w": weights,
        "x_in": per_feature(np.concatenate([I["x_prompt"][0], I["x_sample"].reshape(S, D_MODEL)])),
        "params": params, "consts": consts, "att_consts": att,
        "dt_params": np.stack([I["ssm_dt_bias"][0], I["ssm_a_log"][0]], 1),
        "conv_state": I["state_conv"][0].reshape(DEC_BATCH, CONV - 1, NXBC, P).transpose(3, 2, 0, 1),
        "ssm_state": state, "ssm_state_t": state.transpose(3, 1, 0, 2),
        "cache_kt": cache_k.transpose(3, 2, 0, 1),
        "cache_v": cache_v.reshape(DEC_BATCH, WINDOW, -1).transpose(1, 0, 2),
        "cache_kv": np.stack([cache_k, cache_v]).reshape(2, DEC_BATCH, WINDOW, -1),
    }
    arrays = {k: np.ascontiguousarray(v) for k, v in arrays.items()}
    outs = {"y": (P, NK, T), "ssm_p": (NX, P, D_STATE), "ssm_s": (DEC_BATCH, NX, P, D_STATE),
            "conv_p": (P, NXBC, CONV - 1), "conv_s": (P, NXBC, DEC_BATCH, CONV - 1), "kwin_p": (WINDOW, KVH * HD),
            "vwin_p": (WINDOW, KVH * HD), "kv_kept": (2, DEC_BATCH, WINDOW - DEC_SEQ, KVH * HD),
            "kv_new": (S, 2 * KVH * HD)}
    nc = bacc.Bacc("TRN2", target_bir_lowering=False, num_devices=1)
    build(nc, *[nc.dram_tensor(n, v.shape, F32, kind="ExternalInput").ap() for n, v in arrays.items()],
          *[nc.dram_tensor(n, v, F32, kind="ExternalOutput").ap() for n, v in outs.items()])
    r = run_bass_kernel_spmd(nc, [arrays], core_ids=[0]).results[0]

    y = r["y"].transpose(2, 1, 0).reshape(T, D_MODEL)
    heads = (1, DEC_BATCH, HEADS, HEAD_DIM, D_STATE)
    new = r["kv_new"].reshape(DEC_BATCH, DEC_SEQ, 2, KVH * HD).transpose(2, 0, 1, 3)
    k_s, v_s = np.concatenate([r["kv_kept"], new], 2).reshape(2, DEC_BATCH, WINDOW, KVH, HD)
    return (y[:SEQ].reshape(1, SEQ, D_MODEL), y[SEQ:].reshape(DEC_BATCH, DEC_SEQ, D_MODEL),
            r["ssm_p"].reshape((1, 1) + heads[2:]), r["conv_p"].transpose(2, 1, 0).reshape(1, 1, CONV - 1, P * NXBC),
            r["kwin_p"].reshape(1, WINDOW, KVH, HD), r["vwin_p"].reshape(1, WINDOW, KVH, HD),
            r["ssm_s"].reshape(heads), r["conv_s"].transpose(2, 3, 1, 0).reshape(1, DEC_BATCH, CONV - 1, P * NXBC),
            k_s, v_s)
```
